# Optimizing a Trainium2 kernel written in Bass

```python
import jax, jax.numpy as jnp
from jax import lax
import numpy as np

D_MODEL = 1024
BATCH = 1
SEQ = 256
DEPTH = 1

GRID_W = 64
CTX_LEN = 256
N_MIXERS = 2
N_HEADS = 16
HEAD_DIM = D_MODEL // N_HEADS
NA_MAX_ROWS = 8
NA_COLS = 16
POOL_SIZES = (2, 4, 8, 16)
N_POOL_GROUPS = len(POOL_SIZES)
POOL_GROUP_DIM = D_MODEL // N_POOL_GROUPS
N_EXPERTS = 32
TOP_K = 4
D_EXPERT = D_MODEL
SWIGLU_LIMIT = 7.0
SWIGLU_ALPHA = 1.702
RMS_EPS = 1e-6
N_ATTN_LAYERS = (DEPTH + N_MIXERS - 1) // N_MIXERS
N_POOL_LAYERS = DEPTH // N_MIXERS

kernel_name = 'hybrid_natten_pool_moe_dit'

def rms_norm(x, g):
    xf = x.astype(jnp.float32)
    y = xf * lax.rsqrt(jnp.mean(xf * xf, axis=-1, keepdims=True) + RMS_EPS)
    return (y * g.astype(jnp.float32)).astype(x.dtype)

def adaln(cond, w, b):
    mod = jax.nn.silu(cond) @ w + b
    return jnp.split(mod, 6, axis=-1)

def modulate(x, g, shift, scale):
    return rms_norm(x, g) * (1 + scale) + shift

def neighbourhood_attention(q, k, v, k_ctx, v_ctx, rpb):
    B, L, H, Dh = q.shape
    rows = L // GRID_W
    kh = min(NA_MAX_ROWS, rows)
    kw = NA_COLS
    q = q * (Dh ** -0.5)
    qg = q.reshape(B, rows, GRID_W, H, Dh).transpose(1, 0, 2, 3, 4)
    kg = k.reshape(B, rows, GRID_W, H, Dh)
    vg = v.reshape(B, rows, GRID_W, H, Dh)
    r_idx = jnp.arange(rows)
    row_start = jnp.clip(r_idx - kh // 2, 0, rows - kh)
    c_idx = jnp.arange(GRID_W)
    col_start = jnp.clip(c_idx - kw // 2, 0, GRID_W - kw)
    col_win = col_start[:, None] + jnp.arange(kw)[None, :]
    dc = col_win - c_idx[:, None] + (NA_COLS - 1)

    def row_block(args):
        q_r, r, r0 = args
        k_blk = lax.dynamic_slice_in_dim(kg, r0, kh, axis=1)
        v_blk = lax.dynamic_slice_in_dim(vg, r0, kh, axis=1)
        k_win = k_blk[:, :, col_win]
        v_win = v_blk[:, :, col_win]
        dr = r0 + jnp.arange(kh) - r + (NA_MAX_ROWS - 1)
        bias = rpb[:, dr[:, None, None], dc[None, :, :]]
        s_loc = jnp.einsum('bchd,bicjhd->bhcij', q_r, k_win, preferred_element_type=jnp.float32)
        s_loc = s_loc + bias.transpose(0, 2, 1, 3)[None].astype(jnp.float32)
        s_loc = s_loc.reshape(B, H, GRID_W, kh * kw)
        s_ctx = jnp.einsum('bchd,bnhd->bhcn', q_r, k_ctx, preferred_element_type=jnp.float32)
        p = jax.nn.softmax(jnp.concatenate([s_loc, s_ctx], axis=-1), axis=-1).astype(v.dtype)
        p_loc = p[..., :kh * kw].reshape(B, H, GRID_W, kh, kw)
        p_ctx = p[..., kh * kw:]
        return (jnp.einsum('bhcij,bicjhd->bchd', p_loc, v_win)
                + jnp.einsum('bhcn,bnhd->bchd', p_ctx, v_ctx))

    o = lax.map(row_block, (qg, r_idx, row_start))
    return o.transpose(1, 0, 2, 3, 4).reshape(B, L, H * Dh)

def context_attention(q, k, v):
    B, C, H, Dh = q.shape
    s = jnp.einsum('bqhd,bkhd->bhqk', q * (Dh ** -0.5), k, preferred_element_type=jnp.float32)
    p = jax.nn.softmax(s, axis=-1).astype(v.dtype)
    return jnp.einsum('bhqk,bkhd->bqhd', p, v).reshape(B, C, H * Dh)

def multiscale_pool(h, w, b, scale):
    B, L, D = h.shape
    hf = h.astype(jnp.float32)
    csum = jnp.concatenate([jnp.zeros((B, 1, D), jnp.float32), jnp.cumsum(hf, axis=1)], axis=1)
    t = jnp.arange(L)
    diffs = []
    for g, size in enumerate(POOL_SIZES):
        sl = slice(g * POOL_GROUP_DIM, (g + 1) * POOL_GROUP_DIM)
        lo = jnp.clip(t - size // 2, 0, L)
        hi = jnp.clip(t - size // 2 + size, 0, L)
        cnt = (hi - lo).astype(jnp.float32)[None, :, None]
        mean = (csum[:, hi, sl] - csum[:, lo, sl]) / cnt
        diffs.append(mean - hf[:, :, sl])
    diff = jnp.stack(diffs, axis=2).astype(h.dtype)
    y = jnp.einsum('blgc,gcd->blgd', diff, w) + b
    return y.reshape(B, L, D) * scale

def moe(x, w_router, b_router, w_up, b_up, w_down, b_down):
    B, L, D = x.shape
    xt = x.reshape(B * L, D)
    logits = (xt @ w_router + b_router).astype(jnp.float32)
    top_v, top_i = lax.top_k(logits, TOP_K)
    top_w = jax.nn.softmax(top_v, axis=-1)
    gates = jnp.sum(jax.nn.one_hot(top_i, N_EXPERTS, dtype=jnp.float32) * top_w[..., None], axis=1)
    out = jnp.zeros((B * L, D), jnp.float32)
    for e in range(N_EXPERTS):
        hid = xt @ w_up[e] + b_up[e]
        x_glu = jnp.minimum(hid[:, :D_EXPERT], SWIGLU_LIMIT)
        x_lin = jnp.clip(hid[:, D_EXPERT:], -SWIGLU_LIMIT, SWIGLU_LIMIT)
        act = x_glu * jax.nn.sigmoid(SWIGLU_ALPHA * x_glu) * (x_lin + 1)
        y = act @ w_down[e] + b_down[e]
        out = out + gates[:, e:e + 1] * y.astype(jnp.float32)
    return out.astype(x.dtype).reshape(B, L, D)

def setup_inputs(seed: int = 0) -> dict:
    key = jax.random.key(seed)
    ks = jax.random.split(key, 20)
    f32 = jnp.float32
    D = D_MODEL
    nrm = lambda k, shape, s: jax.random.normal(k, shape, f32) * s
    return {
        'x': nrm(ks[0], (BATCH, SEQ, D), 1.0),
        'c': nrm(ks[1], (BATCH, D), 1.0),
        'ctx': nrm(ks[2], (BATCH, CTX_LEN, D), 1.0),
        'c_ctx': nrm(ks[3], (D,), 1.0),
        'ada_w': nrm(ks[4], (DEPTH, D, 6 * D), 0.5 * D ** -0.5),
        'ada_b': nrm(ks[5], (DEPTH, 6 * D), 0.02),
        'norm_g': 1.0 + nrm(ks[6], (DEPTH, 4, D), 0.05),
        'na_w_qkv': nrm(ks[7], (N_ATTN_LAYERS, D, 3 * D), D ** -0.5),
        'na_w_o': nrm(ks[8], (N_ATTN_LAYERS, D, D), D ** -0.5),
        'na_rpb': nrm(ks[9], (N_ATTN_LAYERS, N_HEADS, 2 * NA_MAX_ROWS - 1, 2 * NA_COLS - 1), 0.1),
        'pool_w': nrm(ks[10], (N_POOL_LAYERS, N_POOL_GROUPS, POOL_GROUP_DIM, POOL_GROUP_DIM), POOL_GROUP_DIM ** -0.5),
        'pool_b': nrm(ks[11], (N_POOL_LAYERS, N_POOL_GROUPS, POOL_GROUP_DIM), 0.02),
        'pool_scale': 1.0 + nrm(ks[12], (N_POOL_LAYERS, D), 0.1),
        'moe_w_router': nrm(ks[13], (DEPTH, D, N_EXPERTS), D ** -0.5),
        'moe_b_router': nrm(ks[14], (DEPTH, N_EXPERTS), 0.01),
        'moe_w_up': nrm(ks[15], (DEPTH, N_EXPERTS, D, 2 * D_EXPERT), D ** -0.5),
        'moe_b_up': nrm(ks[16], (DEPTH, N_EXPERTS, 2 * D_EXPERT), 0.02),
        'moe_w_down': nrm(ks[17], (DEPTH, N_EXPERTS, D_EXPERT, D), D_EXPERT ** -0.5),
        'moe_b_down': nrm(ks[18], (DEPTH, N_EXPERTS, D), 0.02),
    }

def reference(x, c, ctx, c_ctx, ada_w, ada_b, norm_g, na_w_qkv, na_w_o, na_rpb, pool_w, pool_b, pool_scale,
              moe_w_router, moe_b_router, moe_w_up, moe_b_up, moe_w_down, moe_b_down):
    B, L, D = x.shape
    C = ctx.shape[1]
    h_ctx = ctx
    for i in range(DEPTH):
        mixer = i % N_MIXERS
        ctx_needed = any(j % N_MIXERS == 0 for j in range(i + 1, DEPTH))
        sh1, sc1, g1, sh2, sc2, g2 = [m[:, None, :] for m in adaln(c, ada_w[i], ada_b[i])]
        if mixer == 0 or ctx_needed:
            csh1, csc1, cg1, csh2, csc2, cg2 = adaln(c_ctx, ada_w[i], ada_b[i])
            hc = modulate(h_ctx, norm_g[i, 0], csh1, csc1)
        hx = modulate(x, norm_g[i, 0], sh1, sc1)
        if mixer == 0:
            a = i // N_MIXERS
            qkv_x = (hx @ na_w_qkv[a]).reshape(B, L, 3, N_HEADS, HEAD_DIM)
            qkv_c = (hc @ na_w_qkv[a]).reshape(B, C, 3, N_HEADS, HEAD_DIM)
            q, k, v = qkv_x[:, :, 0], qkv_x[:, :, 1], qkv_x[:, :, 2]
            qc, kc, vc = qkv_c[:, :, 0], qkv_c[:, :, 1], qkv_c[:, :, 2]
            mx = neighbourhood_attention(q, k, v, kc, vc, na_rpb[a]) @ na_w_o[a]
            if ctx_needed:
                mc = context_attention(qc, kc, vc) @ na_w_o[a]
        else:
            p = i // N_MIXERS
            mx = multiscale_pool(hx, pool_w[p], pool_b[p], pool_scale[p])
            if ctx_needed:
                mc = multiscale_pool(hc, pool_w[p], pool_b[p], pool_scale[p])
        x = x + g1 * rms_norm(mx, norm_g[i, 1])
        hx2 = modulate(x, norm_g[i, 2], sh2, sc2)
        if ctx_needed:
            h_ctx = h_ctx + cg1 * rms_norm(mc, norm_g[i, 1])
            hc2 = modulate(h_ctx, norm_g[i, 2], csh2, csc2)
            f_all = moe(jnp.concatenate([hx2, hc2], axis=1), moe_w_router[i], moe_b_router[i],
                        moe_w_up[i], moe_b_up[i], moe_w_down[i], moe_b_down[i])
            fx, fc = f_all[:, :L], f_all[:, L:]
            h_ctx = h_ctx + cg2 * rms_norm(fc, norm_g[i, 3])
        else:
            fx = moe(hx2, moe_w_router[i], moe_b_router[i], moe_w_up[i], moe_b_up[i],
                     moe_w_down[i], moe_b_down[i])
        x = x + g2 * rms_norm(fx, norm_g[i, 3])
    return x


_drawn_inputs = setup_inputs


def setup_inputs(seed=0):
    import zlib

    import numpy as np

    out = dict(_drawn_inputs(seed))
    spreads = {}
    factors = {'na_rpb': 4.332, 'moe_b_up': 8.0, 'moe_b_down': 8.0, 'moe_b_router': 2.778}
    for name, (base, spread) in spreads.items():
        noise = np.random.default_rng([zlib.crc32(name.encode()), seed]).standard_normal(out[name].shape)
        drawn = base * np.exp(spread * noise) if base else spread * noise
        out[name] = __import__('jax').numpy.asarray(drawn.astype(out[name].dtype))
    for name, factor in factors.items():
        out[name] = (out[name] * factor).astype(out[name].dtype)
    return out
```

```python
from contextlib import ExitStack

import concourse.bass as bass
import numpy as np
from concourse import mybir
from concourse.alu_op_type import AluOpType as ALU

F32 = mybir.dt.float32
BF16 = mybir.dt.bfloat16
I32 = mybir.dt.int32
ACT = mybir.ActivationFunctionType
AX = mybir.AxisListType

P = 128
D = 1024
TOK = 256
CTX = 256
KC = D // P
HEADS, HD = 16, 64
GRID_W, ROWS, WIN = 64, 4, 16
RPB_ROWS, RPB_COLS = 15, 31
E, TOPK = 32, 4
SLOTS = 64
MAX_EXTRA = (TOK * TOPK) // SLOTS - 1
NCOL = E + MAX_EXTRA + 1
EPS = 1e-6
NEG = -1.0e30
LIMIT, ALPHA = 7.0, 1.702
HALF = 512

RING = 12
ADA0, QK, VV, ADA1, ADA2, WO, EXP = 0, 8, 16, 20, 28, 36, 40
PER = 12
BIAS_SLOTS = 8


def build(nc, x, c, ctx_in, c_ctx, ada_w, ada_b, norm_g, w_qkv, w_o, rpb, w_router, b_router,
          w_up, b_up, w_down, b_down, out):
    with ExitStack() as st:
        def sb(name, shape, dt=F32):
            return st.enter_context(nc.sbuf_tensor(name, shape, dt))

        def sem(name):
            return st.enter_context(nc.semaphore(name))

        bank = [st.enter_context(nc.psum_tensor(f"bank{i}", [P, HALF], F32)) for i in range(8)]

        ring = sb("ring", [P, RING, 2048])
        tokens = sb("tokens", [P, 4, D])
        bias = tokens[:, :, :].rearrange("p a (b c) -> p (a b) c", c=512)
        hT_mem = sb("hT_mem", [P, KC * 512])
        hT = hT_mem[:, :].rearrange("p (k t) -> p k t", k=KC)
        oT = hT_mem[:, 0:2048].rearrange("p (k t) -> p k t", k=KC)
        acc = hT_mem[:, 2048:4096].rearrange("p (t d) -> p t d", t=2)
        kT_mem = sb("kT_mem", [P, KC * 512])
        kT = kT_mem[:, :].rearrange("p (k t) -> p k t", k=KC)
        x1 = kT_mem[:, 0:2048].rearrange("p (t d) -> p t d", t=2)
        h2T = kT_mem[:, 2048:4096].rearrange("p (k t) -> p k t", k=KC)
        q_mem = sb("q_mem", [P, KC * TOK])
        qT = q_mem[:, :].rearrange("p (k t) -> p k t", k=KC)
        h2 = q_mem[:, :].rearrange("p (t d) -> p t d", t=2)
        v_mem = sb("v_mem", [P, 4 * D])
        v = v_mem[:, :].rearrange("p (t d) -> p t d", t=4)
        xT = v_mem[:, 0:512].rearrange("p (j s) -> p j s", j=4)
        glu = v_mem[:, 512:1024]
        lin = v_mem[:, 1024:1536]
        sig = v_mem[:, 1536:2048]
        act = v_mem[:, 2048:2560]
        aT = v_mem[:, 2560:3072].rearrange("p (j s) -> p j s", j=4)
        y = v_mem[:, 3072:3584]
        combT = v_mem[:, 3584:3840].rearrange("p (t s) -> p t s", t=2)
        tmp = v_mem[:, 0:2048].rearrange("p (t d) -> p t d", t=2)
        junk = v_mem[:, 2048:3072]
        mod = [sb(f"mod{i}", [P, D]) for i in range(4)]
        scale1, shift1, cscale1, cshift1 = mod
        gate1, shift2, scale2, gate2 = mod
        probs_mem = mod[2], mod[3]
        probs = [m[:, 512 * i:512 * i + 512] for m in probs_mem for i in range(2)]
        gain = sb("gain", [P, D])
        adab = sb("adab", [P, 3, HALF])
        rows = sb("rows", [P, HALF])
        pT_mem = sb("pT_mem", [P, 1024])
        probsT = pT_mem[:, :].rearrange("p (u k t) -> p u k t", u=2, k=4)
        wtmp = pT_mem[:, 0:2 * GRID_W].rearrange("p (i c) -> p i c", i=2)
        crow, csig = pT_mem[0:2 * KC, 768:896], pT_mem[0:2 * KC, 896:1024]
        small = pT_mem[:, 0:12 * E].rearrange("p (i e) -> p i e", e=E)
        pick = pT_mem[:, 384:512].rearrange("p (t s) -> p t s", t=2)
        gT = pT_mem[0:E, 768:768 + TOK]
        comb = pT_mem[:, 512:768].rearrange("p (t a s) -> p t a s", t=2, a=2)
        ident = sb("ident", [P, P])
        ones = sb("ones", [P, P])
        before = sb("before", [P, P])
        sel = sb("sel", [P, 2, P])
        pmod = sb("pmod", [P, 1])
        slot_no = sb("slot_no", [P, 2, SLOTS])
        qcol = sb("qcol", [P, 1])
        wmask = sb("wmask", [P, GRID_W])
        neghalf = sb("neghalf", [P, 1])
        condT = sb("condT", [P, KC, 32])
        ssq = sb("ssq", [P, 4])
        ssq2 = sb("ssq2", [P, 2, 2])
        ssq3 = sb("ssq3", [P, 2])
        ssq4 = sb("ssq4", [P, 2])
        ms = sb("ms", [P, 4, 4])
        rstd = sb("rstd", [P, 4, 4])
        nmax = sb("nmax", [P, 4])
        psum_p = sb("psum_p", [P, 4])
        rinv = sb("rinv", [P, 4])
        wr = sb("wr", [P, KC, E])
        br = sb("br", [P, E])
        bup = tokens[0:E, 0:2, :].rearrange("p a d -> p (a d)")
        xe = tokens[:, 0, 0:HALF]
        bup_parts = tokens[:, 2, :].bitcast(BF16)[0:3 * E, :]
        bup_part = hT_mem[0:E, 2048:3072].bitcast(BF16)
        bdown = tokens[0:E, 3, :]
        rank_e, gate_e2 = small[:, 0:2, :], small[:, 4:6, :]
        rT, blocks, first = mod[1][0:E, 0:TOK], mod[1][0:E, 256:260], mod[1][0:E, 260:261]
        owner, base, place, inside = (mod[1][0:E, a:a + NCOL] for a in (320, 384, 448, 512))
        owner3 = mod[1][0:3 * E, 576:576 + NCOL]
        bsel = mod[1][0:3 * E, 640:640 + SLOTS // 2].bitcast(BF16)
        rank_col = sb("rank_col", [P, 2, NCOL])
        gate_col = sb("gate_col", [P, 2, NCOL])
        block_no = sb("block_no", [E, NCOL])
        whose_i = sb("whose_i", [1, NCOL], I32)
        ends_i = sb("ends_i", [1, E], I32)

        slot_in = [sem(f"slot_in{i}") for i in range(RING)]
        ring_free = sem("ring_free")
        in_c, in_adab, in_x, in_ctx = sem("in_c"), sem("in_adab"), sem("in_x"), sem("in_ctx")
        in_router, in_gain, in_res = sem("in_router"), sem("in_gain"), sem("in_res")
        in_bdown, in_bup, out_done = sem("in_bdown"), sem("in_bup"), sem("out_done")
        in_bias = [sem(f"in_bias{i}") for i in range(BIAS_SLOTS)]
        pool_step = sem("pool_step")
        consts = sem("consts")
        dve_step = sem("dve_step")
        adab_zero = sem("adab_zero")
        c_sig, c_silu, c_T, cond_ready = sem("c_sig"), sem("c_silu"), sem("c_T"), sem("cond_ready")
        rows_ready, bc_done = sem("rows_ready"), sem("bc_done")
        bc_dve, bc_act = sem("bc_dve"), sem("bc_act")
        ssq_ready, ms_ready, rstd_ready = sem("ssq_ready"), sem("ms_ready"), sem("rstd_ready")
        mod_ready, tr_done, tr_act = sem("mod_ready"), sem("tr_done"), sem("tr_act")
        proj_done, proj_act, proj_dve = sem("proj_done"), sem("proj_act"), sem("proj_dve")
        bias_ready, bias_used = sem("bias_ready"), sem("bias_used")
        s_done, max_ready, exp_ready = sem("s_done"), sem("max_ready"), sem("exp_ready")
        sum_inv, prob_ready, pT_done, pT_ready = sem("sum_inv"), sem("prob_ready"), sem("pT_done"), sem("pT_ready")
        o_done, o_ready = sem("o_done"), sem("o_ready")
        wo_done, x1_ready, h2_ready = sem("wo_done"), sem("x1_ready"), sem("h2_ready")
        h2T_done, h2T_ready, logit_done = sem("h2T_done"), sem("h2T_ready"), sem("logit_done")
        mx_used = sem("mx_used")
        exp_gate_in, exp_gate = sem("exp_gate_in"), sem("exp_gate")
        mask_ready, gates_ready, rank_done = sem("mask_ready"), sem("gates_ready"), sem("rank_done")
        gT_done, gT_ready = sem("gT_done"), sem("gT_ready")
        counts_done, blocks_ready, first_done = sem("counts_done"), sem("blocks_ready"), sem("first_done")
        owner_ready, rT_done, rT_ready, tables_done = sem("owner_ready"), sem("rT_done"), sem("rT_ready"), sem("tables_done")
        tables_ready, rank_ready, bsel_ready, bup_split = sem("tables_ready"), sem("rank_ready"), sem("bsel_ready"), sem("bup_split")
        xe_ready, xeT_done = sem("xe_ready"), sem("xeT_done")
        pick_ready, comb_ready = sem("pick_ready"), sem("comb_ready")
        gather_done, xT_ready, combT_done, combT_ready = sem("gather_done"), sem("xT_ready"), sem("combT_done"), sem("combT_ready")
        up_done, glu_ready, lin_ready = sem("up_done"), sem("glu_ready"), sem("lin_ready")
        sig_ready, pre_ready, act_ready = sem("sig_ready"), sem("pre_ready"), sem("act_ready")
        aT_low, aT_high, aT_dve, aT_act = sem("aT_low"), sem("aT_high"), sem("aT_dve"), sem("aT_act")
        y_ready = sem("y_ready")
        part_done, acc_done = sem("part_done"), sem("acc_done")
        fin_ready = sem("fin_ready")

        def uses_before(slot):
            return len([n for n in range(EXP) if n % RING == slot])

        def chunk_here(eng, n):
            eng.wait_ge(slot_in[n % RING], 16 * (n // RING + 1))

        def expert_chunk_here(eng, e, j):
            s = (EXP + j) % RING
            eng.wait_ge(slot_in[s], e * 16 + 16 * (uses_before(s) + 1))

        def proj_here(eng, i):
            if i == 15:
                eng.wait_ge(ring_free, VV)
            elif i == 23:
                eng.wait_ge(ring_free, ADA1)
            else:
                eng.wait_ge(proj_done, i + 1 - (i > 15))

        def by_row(t):
            return t.rearrange("p (r c) -> p r c", c=GRID_W)

        def backwards(t):
            return by_row(t)[:, :, ::-1]

        def wchunk(n):
            return ring[:, n % RING, :]

        def wpair(n, i):
            return ring[:, (n + i // 2) % RING, D * (i % 2):D * (i % 2) + D]

        def number_of_blocks(eng):
            eng.wait_ge(tables_ready, 1)
            return eng.value_load(ends_i[0:1, E - 1:E], min_val=E, max_val=E + MAX_EXTRA)

        BC0 = [(0, 2), (0, 3), (1, 2), (1, 3), (0, 0), (0, 1), (1, 0), (1, 1)]
        BC1 = [(0, 0), (0, 1), (0, 2), (0, 3)]
        UNITS = [(h, t) for h in range(HEADS) for t in range(2)]
        BD_BANKS = (4, 2, 0, 1)
        ADA2_AT = 8

        block = st.enter_context(nc.Block())

        @block.sync
        def _(sp):
            ada_k = ada_w[0].rearrange("(k p) n -> k p n", p=P)
            qkv_k = w_qkv[0].rearrange("(k p) n -> k p n", p=P)
            v_2k = w_qkv[0].rearrange("(j k p) n -> j p k n", p=P, k=2)
            wo_2k = w_o[0].rearrange("(j k p) n -> j p k n", p=P, k=2)

            def source(n):
                if n < QK:
                    return ada_k[n - ADA0, :, 0:2048]
                if n < VV:
                    return qkv_k[n - QK, :, 0:2048]
                if n < ADA1:
                    return v_2k[n - VV, :, :, 2048:3072]
                if n < ADA2:
                    return ada_k[n - ADA1, :, 2048:4096]
                if n < WO:
                    return ada_k[n - ADA2, :, 4096:6144]
                return wo_2k[n - WO, :, :, :]

            def load(n):
                if n >= RING:
                    sp.wait_ge(ring_free, n - RING + 1)
                src = source(n)
                dst = wchunk(n)
                if len(src.shape) == 3:
                    dst = dst.rearrange("p (k n) -> p k n", k=2)
                sp.dma_start(dst, src).then_inc(slot_in[n % RING], 16)

            def load_bias(h):
                s = h % BIAS_SLOTS
                if h < BIAS_SLOTS:
                    sp.wait_ge(tr_done, 8)
                else:
                    sp.wait_ge(bias_used, 2 * (h - BIAS_SLOTS + 1))
                for r in range(ROWS):
                    first = (h * RPB_ROWS + 7 - r) * RPB_COLS + 15 - (GRID_W - 1)
                    src = bass.AP(rpb.tensor, first, [[1, GRID_W], [RPB_COLS, ROWS], [1, GRID_W]])
                    half = 64 * (r % 2)
                    dst = bias[half:half + 64, s, 256 * (r // 2):256 * (r // 2) + 256]
                    sp.dma_start(dst.rearrange("p (i c) -> p i c", i=ROWS), src).then_inc(in_bias[s], 16)

            for n in range(ADA1):
                load(n)
            for h in range(BIAS_SLOTS):
                load_bias(h)
            for n in range(ADA1, EXP):
                load(n)
            for h in range(BIAS_SLOTS, HEADS):
                load_bias(h)

            up_k = w_up[0].rearrange("e (k p) n -> e k p n", p=P)
            down_2k = w_down[0].rearrange("e (j k p) n -> e j p k n", p=P, k=2)

            def expert(e, blocks_before):
                for j in range(PER):
                    sp.wait_ge(ring_free, blocks_before * PER + (EXP + j - RING + 1))
                    s = (EXP + j) % RING
                    if j < KC:
                        src = up_k[bass.ds(e, 1), j].rearrange("a p n -> (a p) n")
                        sp.dma_start(ring[:, s, :], src).then_inc(slot_in[s], 16)
                    else:
                        src = down_2k[bass.ds(e, 1), j - KC].rearrange("a p k n -> (a p) k n")
                        dst = ring[:, s, :].rearrange("p (k n) -> p k n", k=2)
                        sp.dma_start(dst, src).then_inc(slot_in[s], 16)

            expert(0, 0)
            sp.wait_ge(tables_ready, 1)
            with sp.Fori(1, E) as e:
                blocks_before = sp.value_load(ends_i[0:1, bass.ds(e - 1, 1)], min_val=1, max_val=E + MAX_EXTRA)
                expert(e, blocks_before)
            sp.wait_ge(fin_ready, 2)
            sp.dma_start(out[0].rearrange("(t p) d -> p t d", p=P), tmp).then_inc(out_done, 16)
            sp.wait_ge(out_done, 16)

        @block.gpsimd
        def _(pool):
            g = nc.gpsimd
            n = 0
            pool.dma_start(gain[:, :], norm_g[0][0:1, :].to_broadcast([P, D])).then_inc(in_gain, 16)
            g.memset(ones[:, :], 1.0).then_inc(pool_step, 1)
            g.memset(ident[:, :], 0.0).then_inc(pool_step, 1)
            g.memset(neghalf[:, :], -0.5).then_inc(consts, 1)
            g.iota(slot_no[:, :, :], [[0, 2], [1, SLOTS]], base=0, channel_multiplier=0,
                   allow_small_or_imprecise_dtypes=True).then_inc(consts, 1)
            pool.wait_ge(pool_step, 2)
            for j in range(4):
                pool.wait_ge(consts, 2 + j)
                g.iota(pmod[32 * j:32 * j + 32, :], [[0, 1]], base=0, channel_multiplier=1,
                       allow_small_or_imprecise_dtypes=True).then_inc(consts, 1)
            pool.wait_ge(consts, 6)
            g.iota(block_no[:, :], [[1, NCOL]], base=0, channel_multiplier=0,
                   allow_small_or_imprecise_dtypes=True).then_inc(consts, 1)
            pool.wait_ge(consts, 7)
            g.affine_select(out=ident[:, :], in_=ident[:, :], compare_op=ALU.not_equal, fill=1.0, base=0,
                            pattern=[[-1, P]], channel_multiplier=1).then_inc(consts, 1)
            g.affine_select(out=before[:, :], in_=ones[:, :], compare_op=ALU.is_gt, fill=0.0, base=0,
                            pattern=[[1, P]], channel_multiplier=-1).then_inc(consts, 1)

            def powers(k, cols):
                pool.wait_ge(ms_ready, k + 1)
                g.tensor_tensor(rstd[:, k, 0:cols], ms[:, k, 0:cols], neghalf[:, 0:1].to_broadcast([P, cols]),
                                ALU.pow).then_inc(rstd_ready, 1)

            powers(0, 4)

            pool.wait_ge(consts, 9)
            pool.wait_ge(rstd_ready, 1)
            for j in range(2):
                pool.wait_ge(pool_step, 2 + j)
                g.iota(qcol[64 * j:64 * j + 64, :], [[0, 1]], base=GRID_W - 1, channel_multiplier=-1,
                       allow_small_or_imprecise_dtypes=True).then_inc(pool_step, 1)
            pool.wait_ge(pool_step, 4)
            g.iota(wmask[:, :], [[1, GRID_W]], base=0, channel_multiplier=0,
                   allow_small_or_imprecise_dtypes=True).then_inc(pool_step, 1)
            pool.wait_ge(pool_step, 5)
            g.tensor_scalar(qcol[:, :], qcol[:, :], -float(WIN // 2), 0.0, ALU.add, ALU.max).then_inc(pool_step, 1)
            pool.wait_ge(pool_step, 6)
            g.tensor_scalar(qcol[:, :], qcol[:, :], float(GRID_W - WIN), 0.0, ALU.min, ALU.add).then_inc(pool_step, 1)
            pool.wait_ge(pool_step, 7)
            g.tensor_scalar(wmask[:, :], wmask[:, :], qcol[:, 0:1], None, ALU.subtract).then_inc(pool_step, 1)
            pool.wait_ge(pool_step, 8)
            g.tensor_scalar(wtmp[:, 0, :], wmask[:, :], 0.0, NEG, ALU.is_lt, ALU.mult).then_inc(pool_step, 1)
            g.tensor_scalar(wtmp[:, 1, :], wmask[:, :], float(WIN - 1), NEG, ALU.is_gt, ALU.mult).then_inc(pool_step, 1)
            pool.wait_ge(pool_step, 10)
            g.tensor_tensor(wmask[:, :], wtmp[:, 0, :], wtmp[:, 1, :], ALU.add).then_inc(pool_step, 1)
            pool.wait_ge(pool_step, 11)

            def gain_row(i):
                pool.wait_ge(bc_dve, 2 * i + 2)
                pool.dma_start(gain[:, :], norm_g[0][i:i + 1, :].to_broadcast([P, D])).then_inc(in_gain, 16)

            gain_row(1)
            gain_row(2)

            def mask_bias(h):
                s = h % BIAS_SLOTS
                pool.wait_ge(in_bias[s], 64 * (h // BIAS_SLOTS + 1))
                rows8 = bias[:, s, :].rearrange("p (i c) -> p i c", c=GRID_W)
                g.tensor_tensor(rows8, rows8, wmask[:, :].unsqueeze(1).to_broadcast([P, 8, GRID_W]),
                                ALU.add).then_inc(bias_ready, 1)

            for h in range(BIAS_SLOTS):
                mask_bias(h)
            for u, (h, t) in enumerate(UNITS):
                pool.wait_ge(sum_inv, u + 1)
                g.tensor_scalar(probs[u % 4], probs[u % 4], rinv[:, u % 4:u % 4 + 1], 1.0, ALU.mult,
                                ALU.mult).then_inc(prob_ready, 1)
                if t == 1 and h < HEADS - BIAS_SLOTS:
                    mask_bias(h + BIAS_SLOTS)
            gain_row(3)
            powers(1, 2)
            powers(2, 2)
            powers(3, 2)

        @block.scalar
        def _(sc):
            s = nc.scalar
            sc.dma_start(crow[0:KC, :], c.rearrange("a (k p) -> (a k) p", p=P)).then_inc(in_c, 16)
            sc.dma_start(crow[KC:2 * KC, :], c_ctx.rearrange("(k p) -> k p", p=P)).then_inc(in_c, 16)
            x_t = x[0].rearrange("(t p) d -> p t d", p=P)
            sc.dma_start(tokens[:, 0:2, :], x_t).then_inc(in_x, 16)
            sc.dma_start(tokens[:, 2:4, :], ctx_in[0].rearrange("(t p) d -> p t d", p=P)).then_inc(in_ctx, 16)
            sc.wait_ge(adab_zero, 1)
            for r in range(2):
                sc.dma_start(adab[r:r + 97:32, :, :], ada_b[0].rearrange("(g j n) -> j g n", g=3, j=4)).then_inc(in_adab, 16)
            sc.dma_start(wr[:, :, :], w_router[0].rearrange("(k p) e -> p k e", p=P)).then_inc(in_router, 16)
            sc.dma_start(br[:, :], b_router[0:1, :].to_broadcast([P, E])).then_inc(in_router, 16)

            sc.wait_ge(in_c, 32)
            s.activation(csig, crow, ACT.Sigmoid).then_inc(c_sig, 1)
            sc.wait_ge(c_T, 1)
            sc.wait_ge(cond_ready, 1)
            s.activation(condT[:, :, 0:2], bank[1][:, 0:2 * KC].rearrange("p (r k) -> p k r", r=2),
                         ACT.Copy).then_inc(cond_ready, 1)
            for t in range(4):
                sc.wait_ge(in_x if t < 2 else in_ctx, 16)
                s.activation(hT_mem[:, D * t:D * t + D], tokens[:, t, :], ACT.Square,
                             accum_out=ssq[:, t:t + 1]).then_inc(ssq_ready, 1)
            for i in range(4, 8):
                sc.wait_ge(bc_done, i + 1)
                dst = (shift1, cshift1)[i // 2 - 2]
                s.activation(dst[:, HALF * (i % 2):HALF * (i % 2) + HALF], bank[i][:, :], ACT.Copy).then_inc(bc_act, 1)
            for i in range(8):
                sc.wait_ge(tr_done, i + 1)
                t, k0 = i // 2, 4 * (i % 2)
                s.activation(hT[:, k0:k0 + 4, P * t:P * t + P], bank[i][:, :].rearrange("p (k t) -> p k t", k=4),
                             ACT.Copy).then_inc(tr_act, 1)
            for i in range(0, 24, 2):
                proj_here(sc, i)
                if i < 8:
                    s.activation(by_row(qT[:, i, :]), backwards(bank[i % 8][:, 0:TOK]), ACT.Copy, scale=HD ** -0.5).then_inc(proj_act, 1)
                elif i < 16:
                    s.activation(kT[:, i - 8, :], bank[i % 8][:, :], ACT.Copy).then_inc(proj_act, 1)
                else:
                    s.activation(v[:, (i - 16) // 2, 0:HALF], bank[i % 8][:, :], ACT.Copy).then_inc(proj_act, 1)
            for i in range(2):
                sc.wait_ge(bc_done, 8 + 2 + i + 1)
                s.activation(shift2[:, HALF * i:HALF * i + HALF], bank[3 + i][:, :], ACT.Copy).then_inc(bc_act, 1)

            def softmax_exp(u):
                sc.wait_ge(max_ready, u + 1)
                if u >= 4:
                    sc.wait_ge(pT_done, u - 3)
                s.activation(probs[u % 4], bank[u % 3][:, :], ACT.Exp, bias=nmax[:, u % 4:u % 4 + 1],
                             accum_out=psum_p[:, u % 4:u % 4 + 1]).then_inc(exp_ready, 1)

            def take_probsT(u):
                sc.wait_ge(pT_done, u + 1)
                if u >= 2:
                    sc.wait_ge(o_done, u - 1)
                s.activation(probsT[:, u % 2, :, :], bank[3 + u % 2][:, :].rearrange("p (k t) -> p k t", k=4),
                             ACT.Copy).then_inc(pT_ready, 1)

            for u in range(len(UNITS)):
                softmax_exp(u)
                if u >= 1:
                    take_probsT(u - 1)
            take_probsT(len(UNITS) - 1)
            sc.wait_ge(s_done, len(UNITS))
            sc.dma_start(x1, x_t).then_inc(in_res, 16)
            sc.wait_ge(bias_used, len(UNITS))
            sc.dma_start(bup, b_up[0]).then_inc(in_bup, 16)
            sc.dma_start(bdown, b_down[0]).then_inc(in_bdown, 16)
            for t in range(2):
                if t == 0:
                    sc.wait_ge(wo_done, 1)
                else:
                    sc.wait_ge(ring_free, EXP)
                    sc.wait_ge(ssq_ready, 6)
                for i in range(2):
                    s.activation(junk[:, HALF * i:HALF * i + HALF], bank[4 + 2 * t + i][:, :], ACT.Square,
                                 accum_out=ssq2[:, t, i:i + 1]).then_inc(ssq_ready, 1)
            for t in range(2):
                sc.wait_ge(x1_ready, t + 1)
                sc.wait_ge(ssq_ready, 8 + t)
                s.activation(junk, x1[:, t, :], ACT.Square, accum_out=ssq3[:, t:t + 1]).then_inc(ssq_ready, 1)
            for i in range(4):
                sc.wait_ge(h2T_done, i + 1)
                t, k0 = i // 2, 4 * (i % 2)
                s.activation(h2T[:, k0:k0 + 4, P * t:P * t + P], bank[i][:, :].rearrange("p (k t) -> p k t", k=4),
                             ACT.Copy).then_inc(h2T_ready, 1)
            for t in range(2):
                sc.wait_ge(exp_gate_in, t + 1)
                s.activation(small[:, 8 + t, :], small[:, t, :], ACT.Exp, bias=nmax[:, t:t + 1]).then_inc(exp_gate, 1)

            def take_xe(b):
                sc.wait_ge(gather_done, b + 1)
                s.activation(xe, bank[3][:, :], ACT.Copy).then_inc(xe_ready, 1)

            def take_xT(b):
                sc.wait_ge(xeT_done, b + 1)
                s.activation(xT, bank[3][:, :].rearrange("p (j s) -> p j s", j=4), ACT.Copy).then_inc(xT_ready, 1)

            sc.wait_ge(gT_done, 1)
            s.activation(gT, bank[7][0:E, 0:TOK], ACT.Copy).then_inc(gT_ready, 1)
            sc.wait_ge(bup_split, 1)
            take_xe(0)
            sc.wait_ge(rT_done, 1)
            s.activation(rT, bank[7][0:E, 0:TOK], ACT.Copy).then_inc(rT_ready, 1)
            take_xT(0)
            for i in range(4):
                sc.wait_ge(part_done, i + 1)
                s.activation(acc[:, i // 2, HALF * (i % 2):HALF * (i % 2) + HALF], bank[BD_BANKS[i]][:, :],
                             ACT.Copy).then_inc(acc_done, 1)

            def block_step(b, is_first=False):
                sc.wait_ge(glu_ready, b + 1)
                s.activation(sig, glu, ACT.Sigmoid, scale=ALPHA).then_inc(sig_ready, 1)
                take_xe(b + 1)
                sc.wait_ge(combT_done, b + 1)
                if not is_first:
                    sc.wait_ge(part_done, b * 4 + 4)
                s.activation(combT, bank[4][:, 0:TOK].rearrange("p (t s) -> p t s", t=2), ACT.Copy).then_inc(combT_ready, 1)
                sc.wait_ge(aT_high, b + 1)
                s.activation(aT[:, 2:4, :], bank[4][:, 0:TOK].rearrange("p (j s) -> p j s", j=2),
                             ACT.Copy).then_inc(aT_act, 1)
                take_xT(b + 1)
                sc.wait_ge(ring_free, b * PER + (EXP + PER))
                s.activation(y, bank[2][:, :], ACT.Copy).then_inc(y_ready, 1)

            block_step(0, is_first=True)
            last_block = number_of_blocks(sc)
            with sc.Fori(1, last_block) as b:
                block_step(b)
            sc.wait_ge(acc_done, last_block * 4 + 4)
            for t in range(2):
                sc.wait_ge(ssq_ready, 10 + t)
                s.activation(junk, acc[:, t, :], ACT.Square,
                             accum_out=ssq4[:, t:t + 1]).then_inc(ssq_ready, 1)

        @block.vector
        def _(ve):
            d = nc.vector
            steps = [0]

            def step(ins):
                ins.then_inc(dve_step, 1)
                steps[0] += 1
                ve.wait_ge(dve_step, steps[0])

            d.memset(adab[:, :, :], 0.0).then_inc(adab_zero, 1)
            d.memset(condT[:, :, :], 0.0).then_inc(cond_ready, 1)
            ve.wait_ge(c_sig, 1)
            d.tensor_tensor(csig, csig, crow, ALU.mult).then_inc(c_silu, 1)
            ve.wait_ge(pool_step, 2)
            ve.wait_ge(consts, 9)
            d.tensor_scalar(sel[:, 0, :], ones[:, :], 1.0, pmod[:, 0:1], ALU.subtract, ALU.is_equal)
            step(d.tensor_scalar(sel[:, 1, :], ones[:, :], pmod[:, 0:1], None, ALU.is_equal))

            def mean_squares(k, src, cols):
                d.tensor_scalar(ms[:, k, 0:cols], src, 1.0 / D, EPS, ALU.mult, ALU.add).then_inc(ms_ready, 1)

            ve.wait_ge(ssq_ready, 4)
            mean_squares(0, ssq[:, :], 4)

            def take_rows(g):
                ve.wait_ge(ring_free, (ADA0, ADA1, ADA2)[g] + KC)
                if g == 0:
                    ve.wait_ge(in_adab, 32)
                else:
                    ve.wait_ge(bc_done, (8, 12)[g - 1])
                b = (0, 0, 7)[g]
                d.tensor_tensor(rows[:, :], bank[b][:, :], adab[:, g, :], ALU.add).then_inc(rows_ready, 1)

            take_rows(0)
            ve.wait_ge(in_gain, 16)
            for i in range(4):
                ve.wait_ge(bc_done, i + 1)
                h = slice(HALF * (i % 2), HALF * (i % 2) + HALF)
                d.scalar_tensor_tensor((scale1, cscale1)[i // 2][:, h], bank[i][:, :], 1.0, gain[:, h],
                                       ALU.add, ALU.mult).then_inc(bc_dve, 1)
            ve.wait_ge(bc_dve, 4)
            ve.wait_ge(rstd_ready, 1)
            for t in range(4):
                step(d.scalar_tensor_tensor(tokens[:, t, :], tokens[:, t, :], rstd[:, 0, t:t + 1],
                                            (scale1, cscale1)[t // 2][:, :], ALU.mult, ALU.mult))
                ve.wait_ge(bc_act, 2 * (t // 2 + 1))
                d.tensor_tensor(tokens[:, t, :], tokens[:, t, :], (shift1, cshift1)[t // 2][:, :],
                                ALU.add).then_inc(mod_ready, 1)
            for i in range(1, 24, 2):
                proj_here(ve, i)
                if i < 8:
                    d.tensor_scalar(by_row(qT[:, i, :]), backwards(bank[i % 8][:, 0:TOK]), HD ** -0.5, None, ALU.mult).then_inc(proj_dve, 1)
                elif i < 16:
                    d.tensor_copy(kT[:, i - 8, :], bank[i % 8][:, :]).then_inc(proj_dve, 1)
                else:
                    d.tensor_copy(v[:, (i - 16) // 2, HALF:D], bank[i % 8][:, :]).then_inc(proj_dve, 1)
            take_rows(1)
            ve.wait_ge(in_gain, 32)
            for i in range(2):
                ve.wait_ge(bc_done, 8 + i + 1)
                h = slice(HALF * i, HALF * i + HALF)
                d.tensor_tensor(gate1[:, h], bank[1 + i][:, :], gain[:, h], ALU.mult).then_inc(bc_dve, 1)

            def scores(u):
                h, t = UNITS[u]
                ve.wait_ge(s_done, u + 1)
                if t == 0:
                    ve.wait_ge(bias_ready, h + 1)
                sl = bank[u % 3][:, 0:256]
                d.tensor_tensor(sl, sl, bias[:, h % BIAS_SLOTS, 256 * t:256 * t + 256], ALU.add).then_inc(bias_used, 1)
                ve.wait_ge(bias_used, u + 1)
                if u >= 4:
                    ve.wait_ge(exp_ready, u - 3)
                d.tensor_reduce(nmax[:, u % 4:u % 4 + 1], bank[u % 3][:, :], AX.X, ALU.max, negate=True).then_inc(max_ready, 1)

            def invert(u):
                ve.wait_ge(exp_ready, u + 1)
                if u >= 4:
                    ve.wait_ge(prob_ready, u - 3)
                d.reciprocal(rinv[:, u % 4:u % 4 + 1], psum_p[:, u % 4:u % 4 + 1]).then_inc(sum_inv, 1)

            def take_o(h):
                ve.wait_ge(o_done, 2 * h + 2)
                d.tensor_copy(by_row(oT[:, h // 2, :]), backwards(bank[5 + (h // 2) % 2][:, 0:TOK])).then_inc(o_ready, 1)

            for u in range(len(UNITS)):
                scores(u)
                if u >= 1:
                    invert(u - 1)
                if u >= 6 and u % 4 == 2:
                    take_o((u - 6) // 2 + 1)
                if u == ADA2_AT + 1:
                    take_rows(2)
            invert(len(UNITS) - 1)
            take_o(HEADS - 1)
            ve.wait_ge(in_gain, 48)
            for i in range(2):
                ve.wait_ge(bc_done, 12 + i + 1)
                h = slice(HALF * i, HALF * i + HALF)
                d.scalar_tensor_tensor(scale2[:, h], bank[i][:, :], 1.0, gain[:, h], ALU.add, ALU.mult).then_inc(bc_dve, 1)
            ve.wait_ge(in_bup, 16)
            step(d.tensor_copy(bup_parts[0:E, :], bup))
            step(d.tensor_tensor(bup, bup, bup_parts[0:E, :], ALU.subtract))
            step(d.tensor_copy(bup_part, bup))
            step(d.tensor_tensor(bup, bup, bup_part, ALU.subtract))
            d.tensor_copy(bup_parts[E:2 * E, :], bup_part)
            d.tensor_copy(bup_parts[2 * E:3 * E, :], bup).then_inc(bup_split, 1)
            ve.wait_ge(ssq_ready, 8)
            step(d.tensor_tensor(ssq2[:, :, 0], ssq2[:, :, 0], ssq2[:, :, 1], ALU.add))
            mean_squares(1, ssq2[:, :, 0], 2)
            ve.wait_ge(rstd_ready, 2)
            ve.wait_ge(in_res, 16)
            for t in range(2):
                for i in range(2):
                    h = slice(HALF * i, HALF * i + HALF)
                    ins = d.scalar_tensor_tensor(tmp[:, t, h], bank[4 + 2 * t + i][:, :], rstd[:, 1, t:t + 1],
                                                 gate1[:, h], ALU.mult, ALU.mult)
                    ins.then_inc(mx_used, 1)
                ve.wait_ge(mx_used, 2 * t + 2)
                d.tensor_tensor(x1[:, t, :], x1[:, t, :], tmp[:, t, :], ALU.add).then_inc(x1_ready, 1)
            ve.wait_ge(in_gain, 64)
            for i in range(2):
                ve.wait_ge(bc_done, 14 + i + 1)
                h = slice(HALF * i, HALF * i + HALF)
                d.tensor_tensor(gate2[:, h], bank[2 + i][:, :], gain[:, h], ALU.mult).then_inc(bc_dve, 1)
            ve.wait_ge(ssq_ready, 10)
            mean_squares(2, ssq3[:, :], 2)
            ve.wait_ge(rstd_ready, 3)
            for t in range(2):
                step(d.scalar_tensor_tensor(h2[:, t, :], x1[:, t, :], rstd[:, 2, t:t + 1], scale2[:, :], ALU.mult, ALU.mult))
                d.tensor_tensor(h2[:, t, :], h2[:, t, :], shift2[:, :], ALU.add).then_inc(h2_ready, 1)

            logit, top, over, tie, gate_e, mask = (small[:, 2 * i:2 * i + 2, :] for i in range(6))
            ve.wait_ge(in_router, 32)
            for t in range(2):
                ve.wait_ge(logit_done, t + 1)
                step(d.tensor_tensor(logit[:, t, :], bank[4 + t][:, 0:E], br[:, :], ALU.add))
                step(d.max(top[:, t, 0:8], logit[:, t, :]))
                d.tensor_scalar(nmax[:, t:t + 1], top[:, t, 0:1], -1.0, None, ALU.mult).then_inc(exp_gate_in, 1)
                d.tensor_scalar(over[:, t, :], logit[:, t, :], top[:, t, TOPK - 1:TOPK], None, ALU.is_gt)
                step(d.tensor_scalar(tie[:, t, :], logit[:, t, :], top[:, t, TOPK - 1:TOPK], None, ALU.is_equal))
                step(d.tensor_reduce(top[:, t, 8:9], over[:, t, :], AX.X, ALU.add, negate=True))
                d.tensor_scalar(top[:, t, 9:10], top[:, t, 8:9], float(TOPK), None, ALU.add)
                step(d.tensor_tensor_scan(mask[:, t, :], ones[:, 0:E], tie[:, t, :], 0.0, ALU.mult, ALU.add))
                step(d.tensor_scalar(mask[:, t, :], mask[:, t, :], top[:, t, 9:10], None, ALU.is_le))
                step(d.tensor_tensor(mask[:, t, :], mask[:, t, :], tie[:, t, :], ALU.mult))
                d.tensor_tensor(mask[:, t, :], mask[:, t, :], over[:, t, :], ALU.add).then_inc(mask_ready, 1)
                ve.wait_ge(mask_ready, t + 1)
                ve.wait_ge(exp_gate, t + 1)
                step(d.tensor_tensor(gate_e[:, t, :], gate_e[:, t, :], mask[:, t, :], ALU.mult))
                step(d.tensor_reduce(top[:, t, 10:11], gate_e[:, t, :], AX.X, ALU.add))
                step(d.reciprocal(top[:, t, 11:12], top[:, t, 10:11]))
                d.tensor_scalar(gate_e2[:, t, :], gate_e[:, t, :], top[:, t, 11:12], None, ALU.mult).then_inc(gates_ready, 1)
            ve.wait_ge(gates_ready, 2)
            ve.wait_ge(rank_done, 1)
            for t in range(2):
                step(d.scalar_tensor_tensor(rank_e[:, t, :], bank[6][:, E * t:E * t + E], 1.0, mask[:, t, :], ALU.add, ALU.mult))
                d.tensor_scalar(rank_e[:, t, :], rank_e[:, t, :], -1.0, None, ALU.add).then_inc(rank_ready, 1)
            ve.wait_ge(rank_ready, 2)

            def make_pick(ranks, b):
                for t in range(2):
                    ins = d.tensor_scalar(pick[:, t, :], slot_no[:, 0, :], ranks[:, t, bass.ds(b, 1)], None, ALU.is_equal)
                ins.then_inc(pick_ready, 1)

            def make_comb(ranks, gates, b):
                for t in range(2):
                    ins = d.tensor_scalar(comb[:, t, :, :], slot_no[:, :, :], ranks[:, t, bass.ds(b, 1)],
                                          gates[:, t, bass.ds(b, 1)], ALU.is_equal, ALU.mult)
                ins.then_inc(comb_ready, 1)

            def make_bsel(b):
                d.tensor_copy(bsel, owner3[:, bass.ds(b, 1)].to_broadcast([3 * E, SLOTS])).then_inc(bsel_ready, 1)

            make_pick(rank_e, 0)
            ve.wait_ge(counts_done, 1)
            step(d.tensor_copy(blocks[:, 3:4], bank[6][0:E, 0:1]))
            step(d.tensor_scalar(blocks[:, 0:1], blocks[:, 3:4], float(SLOTS), 1.0, ALU.is_gt, ALU.add))
            step(d.tensor_scalar(blocks[:, 1:2], blocks[:, 3:4], float(2 * SLOTS), blocks[:, 0:1], ALU.is_gt, ALU.add))
            d.tensor_scalar(blocks[:, 2:3], blocks[:, 3:4], float(3 * SLOTS), blocks[:, 1:2], ALU.is_gt, ALU.add).then_inc(blocks_ready, 1)
            make_comb(rank_e, gate_e2, 0)
            ve.wait_ge(first_done, 1)
            ve.wait_ge(blocks_ready, 1)
            step(d.tensor_copy(first, bank[6][0:E, 0:1]))
            step(d.tensor_scalar(place, block_no[:, :], first, None, ALU.subtract))
            step(d.tensor_scalar(inside, place, blocks[:, 2:3], None, ALU.is_lt))
            step(d.scalar_tensor_tensor(owner, place, 0.0, inside, ALU.is_ge, ALU.mult))
            d.scalar_tensor_tensor(base, place, -float(SLOTS), owner, ALU.mult, ALU.mult).then_inc(owner_ready, 1)
            for i in range(3):
                ins = d.tensor_copy(owner3[E * i:E * i + E, :], owner)
            step(ins)
            make_bsel(0)
            ve.wait_ge(tables_done, 1)
            d.tensor_copy(whose_i[:, :], bank[6][0:1, 64:64 + NCOL])
            d.tensor_copy(ends_i[:, :], bank[6][0:1, 128:128 + E])
            d.tensor_copy(rank_col[:, :, :], bank[5][:, 0:2 * NCOL].rearrange("p (t b) -> p t b", t=2))
            ins = d.tensor_copy(gate_col[:, :, :], bank[5][:, 2 * NCOL:4 * NCOL].rearrange("p (t b) -> p t b", t=2))
            ins.then_inc(tables_ready, 1)
            ve.wait_ge(tables_ready, 1)

            def add_part(t, b):
                ve.wait_ge(part_done, b * 4 + (2 * t + 2))
                for n in range(2):
                    dst = acc[:, t, HALF * n:HALF * n + HALF]
                    d.tensor_tensor(dst, dst, bank[6 + n][:, :], ALU.add).then_inc(acc_done, 1)

            def block_step(b, is_first=False):
                ve.wait_ge(gather_done, b + 1)
                make_pick(rank_col, b + 1)
                ve.wait_ge(up_done, b + 1)
                d.tensor_scalar(glu, bank[0][:, :], LIMIT, None, ALU.min).then_inc(glu_ready, 1)
                d.tensor_scalar(lin, bank[1][:, :], LIMIT, -LIMIT, ALU.min, ALU.max).then_inc(lin_ready, 1)
                ve.wait_ge(glu_ready, b + 1)
                ve.wait_ge(lin_ready, b + 1)
                d.scalar_tensor_tensor(act, lin, 1.0, glu, ALU.add, ALU.mult).then_inc(pre_ready, 1)
                if not is_first:
                    ve.wait_ge(acc_done, b * 4)
                    add_part(0, b)
                ve.wait_ge(pre_ready, b + 1)
                ve.wait_ge(sig_ready, b + 1)
                d.tensor_tensor(act, act, sig, ALU.mult).then_inc(act_ready, 1)
                make_bsel(b + 1)
                ve.wait_ge(aT_low, b + 1)
                d.tensor_copy(aT[:, 0:2, :], bank[5][:, 0:TOK].rearrange("p (j s) -> p j s", j=2)).then_inc(aT_dve, 1)
                if not is_first:
                    add_part(1, b)
                ve.wait_ge(combT_done, b + 1)
                make_comb(rank_col, gate_col, b + 1)

            block_step(0, is_first=True)
            last_block = number_of_blocks(ve)
            with ve.Fori(1, last_block) as b:
                block_step(b)
            ve.wait_ge(acc_done, last_block * 4)
            add_part(0, last_block)
            add_part(1, last_block)
            ve.wait_ge(ssq_ready, 12)
            mean_squares(3, ssq4[:, :], 2)
            ve.wait_ge(rstd_ready, 4)
            for t in range(2):
                step(d.scalar_tensor_tensor(tmp[:, t, :], acc[:, t, :], rstd[:, 3, t:t + 1], gate2[:, :], ALU.mult, ALU.mult))
                d.tensor_tensor(tmp[:, t, :], tmp[:, t, :], x1[:, t, :], ALU.add).then_inc(fin_ready, 1)

        @block.tensor
        def _(pe):
            mm, tr = nc.tensor.matmul, nc.tensor.transpose

            pe.wait_ge(consts, 9)
            pe.wait_ge(c_silu, 1)
            tr(bank[1][:, 0:2 * KC], csig, ident[0:2 * KC, 0:2 * KC]).then_inc(c_T, 1)
            pe.wait_ge(cond_ready, 2)

            def ada(g, b):
                for k in range(KC):
                    n = (ADA0, ADA1, ADA2)[g] + k
                    chunk_here(pe, n)
                    for j in range(4):
                        last = mm(bank[b][32 * j:32 * j + 32, :], condT[:, k, :], wchunk(n)[:, HALF * j:HALF * j + HALF],
                                  start=k == 0, stop=k == KC - 1)
                    last.then_inc(ring_free, 1)

            def broadcast(jobs, banks):
                for (r, j), b in zip(jobs, banks):
                    mm(bank[b][:, :], sel[32 * j:32 * j + 32, r, :], rows[32 * j:32 * j + 32, :],
                       start=True, stop=True).then_inc(bc_done, 1)

            ada(0, 0)
            pe.wait_ge(dve_step, 1)
            pe.wait_ge(rows_ready, 1)
            broadcast(BC0, range(8))
            pe.wait_ge(bc_dve, 4)
            pe.wait_ge(bc_act, 4)
            for i in range(8):
                t, k0 = i // 2, 4 * (i % 2)
                pe.wait_ge(mod_ready, t + 1)
                for j in range(4):
                    last = tr(bank[i][:, P * j:P * j + P], tokens[:, t, P * (k0 + j):P * (k0 + j) + P], ident[:, :])
                last.then_inc(tr_done, 1)
            for n in range(24):
                if n < 8:
                    pe.wait_ge(tr_act, 8)
                else:
                    pe.wait_ge(proj_act if n % 2 == 0 else proj_dve, (n - 8) // 2 + 1)
                for k in range(KC):
                    if n == 0:
                        chunk_here(pe, QK + k)
                    if n == 16 and k % 2 == 0:
                        chunk_here(pe, VV + k // 2)
                    if n < 8:
                        last = mm(bank[n % 8][:, 0:TOK], wchunk(QK + k)[:, P * n:P * n + P], hT[:, k, 0:TOK],
                                  start=k == 0, stop=k == KC - 1)
                    elif n < 16:
                        last = mm(bank[n % 8][:, :], wchunk(QK + k)[:, P * n:P * n + P], hT[:, k, :],
                                  start=k == 0, stop=k == KC - 1)
                    else:
                        t, i = (n - 16) // 2, n % 2
                        last = mm(bank[n % 8][:, :], hT[:, k, P * t:P * t + P], wpair(VV, k)[:, HALF * i:HALF * i + HALF],
                                  start=k == 0, stop=k == KC - 1)
                    if n == 15 or (n == 23 and k % 2 == 1):
                        last.then_inc(ring_free, 1)
                if n not in (15, 23):
                    last.then_inc(proj_done, 1)
            pe.wait_ge(proj_act, 12)
            pe.wait_ge(proj_dve, 12)
            ada(1, 0)
            pe.wait_ge(rows_ready, 2)
            broadcast(BC1, range(1, 5))

            def score(u):
                h, t = UNITS[u]
                p0 = HD * (h % 2)
                if u >= 3:
                    pe.wait_ge(exp_ready, u - 2)
                mm(bank[u % 3][:, :], qT[p0:p0 + HD, h // 2, P * t:P * t + P], kT[p0:p0 + HD, h // 2, :],
                   start=True, stop=True).then_inc(s_done, 1)

            def transpose_probs(u):
                pe.wait_ge(prob_ready, u + 1)
                if u >= 2:
                    pe.wait_ge(pT_ready, u - 1)
                for kc in range(4):
                    last = tr(bank[3 + u % 2][:, P * kc:P * kc + P], probs[u % 4][:, P * kc:P * kc + P], ident[:, :])
                last.then_inc(pT_done, 1)

            def mix(u):
                h, t = UNITS[u]
                p0 = HD * (h % 2)
                pe.wait_ge(pT_ready, u + 1)
                if h >= 4:
                    pe.wait_ge(o_ready, h // 2 - 1)
                for kc in range(4):
                    last = mm(bank[5 + (h // 2) % 2][p0:p0 + HD, P * t:P * t + P], v[:, kc, HD * h:HD * h + HD],
                              probsT[:, u % 2, kc, :], start=kc == 0, stop=kc == 3)
                last.then_inc(o_done, 1)

            pe.wait_ge(bc_dve, 6)
            pe.wait_ge(bc_act, 6)
            score(0)
            score(1)
            for u in range(len(UNITS)):
                if u == ADA2_AT:
                    ada(2, 7)
                if u + 2 < len(UNITS):
                    score(u + 2)
                transpose_probs(u)
                if u >= 1:
                    mix(u - 1)
            mix(len(UNITS) - 1)

            pe.wait_ge(o_ready, HEADS // 2)
            pe.wait_ge(rows_ready, 3)
            for t in range(2):
                for i in range(2):
                    for k in range(KC):
                        if t == 0 and i == 0 and k % 2 == 0:
                            chunk_here(pe, WO + k // 2)
                        last = mm(bank[4 + 2 * t + i][:, :], oT[:, k, P * t:P * t + P],
                                  wpair(WO, k)[:, HALF * i:HALF * i + HALF], start=k == 0, stop=k == KC - 1)
                        if t == 1 and i == 1 and k % 2 == 1:
                            last.then_inc(ring_free, 1)
                if t == 0:
                    last.then_inc(wo_done, 1)
            broadcast(BC1, range(4))

            pe.wait_ge(bc_dve, 10)
            for i in range(4):
                t, k0 = i // 2, 4 * (i % 2)
                pe.wait_ge(h2_ready, t + 1)
                for j in range(4):
                    last = tr(bank[i][:, P * j:P * j + P], h2[:, t, P * (k0 + j):P * (k0 + j) + P], ident[:, :])
                last.then_inc(h2T_done, 1)
            pe.wait_ge(in_router, 32)
            pe.wait_ge(mx_used, 4)
            for t in range(2):
                pe.wait_ge(h2T_ready, 2 * t + 2)
                for k in range(KC):
                    last = mm(bank[4 + t][:, 0:E], h2T[:, k, P * t:P * t + P], wr[:, k, :], start=k == 0, stop=k == KC - 1)
                last.then_inc(logit_done, 1)
            pe.wait_ge(mask_ready, 2)
            mask = small[:, 10:12, :]
            mm(bank[6][:, 0:E], before[:, :], mask[:, 0, :], start=True, stop=True)
            mm(bank[6][:, E:2 * E], before[:, :], mask[:, 1, :], start=True, stop=False)
            mm(bank[6][:, E:2 * E], ones[:, :], mask[:, 0, :], start=False, stop=True)
            mm(bank[6][:, 2 * E:3 * E], ones[:, :], mask[:, 0, :], start=True, stop=False)
            mm(bank[6][:, 2 * E:3 * E], ones[:, :], mask[:, 1, :], start=False, stop=True).then_inc(rank_done, 1)
            pe.wait_ge(gates_ready, 2)
            for t in range(2):
                last = tr(bank[7][0:E, P * t:P * t + P], gate_e2[:, t, :], ident[:, :])
            last.then_inc(gT_done, 1)

            def gather(b):
                pe.wait_ge(pick_ready, b + 1)
                for t in range(2):
                    for n in range(2):
                        last = mm(bank[3][64 * n:64 * n + 64, :], pick[:, t, :], h2[:, t, HALF * n:HALF * n + HALF],
                                  start=t == 0, stop=t == 1)
                last.then_inc(gather_done, 1)

            def transpose_xe(b):
                pe.wait_ge(xe_ready, b + 1)
                for j in range(4):
                    last = tr(bank[3][:, P * j:P * j + P], xe[:, P * j:P * j + P], ident[:, :])
                last.then_inc(xeT_done, 1)

            gather(0)
            for t in range(2):
                last = mm(bank[6][0:E, 0:1], mask[:, t, :], ones[:, 0:1], start=t == 0, stop=t == 1)
            last.then_inc(counts_done, 1)
            pe.wait_ge(gT_ready, 1)
            pe.wait_ge(in_bdown, 16)
            for i in range(4):
                t, n = i // 2, i % 2
                mm(bank[BD_BANKS[i]][:, :], gT[:, P * t:P * t + P], bdown[:, HALF * n:HALF * n + HALF],
                   start=True, stop=True).then_inc(part_done, 1)
            pe.wait_ge(rank_ready, 2)
            for t in range(2):
                last = tr(bank[7][0:E, P * t:P * t + P], rank_e[:, t, :], ident[:, :])
            last.then_inc(rT_done, 1)
            transpose_xe(0)
            pe.wait_ge(blocks_ready, 1)
            mm(bank[6][0:E, 0:1], before[0:E, 0:E], blocks[:, 2:3], start=True, stop=True).then_inc(first_done, 1)
            pe.wait_ge(owner_ready, 1)
            pe.wait_ge(rT_ready, 1)
            mm(bank[6][0:1, 64:64 + NCOL], pmod[0:E, 0:1], owner, start=True, stop=True)
            mm(bank[6][0:1, 128:128 + E], blocks[:, 2:3], before[0:E, 0:E], start=True, stop=False)
            mm(bank[6][0:1, 128:128 + E], blocks[:, 2:3], ident[0:E, 0:E], start=False, stop=True)
            for t in range(2):
                mm(bank[5][:, NCOL * t:NCOL * t + NCOL], rT[:, P * t:P * t + P], owner, start=True, stop=False)
                mm(bank[5][:, NCOL * t:NCOL * t + NCOL], ones[0:E, :], base, start=False, stop=True)
            for t in range(2):
                last = mm(bank[5][:, NCOL * (2 + t):NCOL * (3 + t)], gT[:, P * t:P * t + P], owner, start=True, stop=True)
            last.then_inc(tables_done, 1)
            pe.wait_ge(acc_done, 4)

            def combine(t, b):
                pe.wait_ge(acc_done, b * 4 + 2 * t)
                for n in range(2):
                    mm(bank[6 + n][:, :], combT[64 * n:64 * n + 64, t, :], y[64 * n:64 * n + 64, :],
                       start=True, stop=True).then_inc(part_done, 1)

            def block_step(b, e, is_first=False):
                pe.wait_ge(xT_ready, b + 1)
                for k in range(KC):
                    expert_chunk_here(pe, e, k)
                    w = ring[:, (EXP + k) % RING, :]
                    for half in range(2):
                        for n in range(2):
                            c0 = D * half + HALF * n
                            last = mm(bank[half][64 * n:64 * n + 64, :], xT[:, k % 4, 64 * (k // 4):64 * (k // 4) + 64],
                                      w[:, c0:c0 + HALF], start=k == 0, stop=False)
                    last.then_inc(ring_free, 1)
                pe.wait_ge(bsel_ready, b + 1)
                for half in range(2):
                    for n in range(2):
                        c0 = D * half + HALF * n
                        last = mm(bank[half][64 * n:64 * n + 64, :], bsel, bup_parts[:, c0:c0 + HALF],
                                  start=False, stop=True)
                last.then_inc(up_done, 1)
                if not is_first:
                    pe.wait_ge(y_ready, b)
                    pe.wait_ge(combT_ready, b)
                    combine(0, b)
                pe.wait_ge(comb_ready, b + 1)
                for t in range(2):
                    last = tr(bank[4][:, P * t:P * t + P], comb[:, t, :, :].rearrange("p a s -> p (a s)"), ident[:, :])
                last.then_inc(combT_done, 1)
                gather(b + 1)
                if not is_first:
                    combine(1, b)
                pe.wait_ge(act_ready, b + 1)
                for j in range(2):
                    last = tr(bank[5][:, P * j:P * j + P], act[:, P * j:P * j + P], ident[:, :])
                last.then_inc(aT_low, 1)
                pe.wait_ge(combT_ready, b + 1)
                for j in range(2):
                    last = tr(bank[4][:, P * j:P * j + P], act[:, P * (2 + j):P * (2 + j) + P], ident[:, :])
                last.then_inc(aT_high, 1)
                transpose_xe(b + 1)
                pe.wait_ge(aT_dve, b + 1)
                pe.wait_ge(aT_act, b + 1)
                for k in range(KC):
                    if k % 2 == 0:
                        expert_chunk_here(pe, e, KC + k // 2)
                    w = ring[:, (EXP + KC + k // 2) % RING, D * (k % 2):D * (k % 2) + D]
                    half, j = k // 4, k % 4
                    for n in range(2):
                        last = mm(bank[2][64 * n:64 * n + 64, :], aT[:, j, 64 * half:64 * half + 64],
                                  w[:, HALF * n:HALF * n + HALF], start=k == 0, stop=k == KC - 1)
                    if k % 2 == 1:
                        last.then_inc(ring_free, 1)

            block_step(0, 0, is_first=True)
            last_block = number_of_blocks(pe)
            with pe.Fori(1, last_block) as b:
                e = pe.value_load(whose_i[0:1, bass.ds(b, 1)], min_val=0, max_val=E - 1)
                block_step(b, e)
            pe.wait_ge(y_ready, last_block)
            pe.wait_ge(combT_ready, last_block)
            combine(0, last_block)
            combine(1, last_block)


_INS = ["x", "c", "ctx", "c_ctx", "ada_w", "ada_b", "norm_g", "na_w_qkv", "na_w_o", "na_rpb", "moe_w_router",
        "moe_b_router", "moe_w_up", "moe_b_up", "moe_w_down", "moe_b_down"]


def kernel(**inputs):
    import concourse.bacc as bacc
    from concourse.bass_utils import run_bass_kernel_spmd

    nc = bacc.Bacc("TRN2", target_bir_lowering=False, num_devices=1)
    arrays, args = {}, []
    for name in _INS:
        a = np.ascontiguousarray(inputs[name])
        arrays[f"in_{name}"] = a
        args.append(nc.dram_tensor(f"in_{name}", a.shape, mybir.dt.from_np(a.dtype), kind="ExternalInput").ap())
    args.append(nc.dram_tensor("out_x", (1, TOK, D), F32, kind="ExternalOutput").ap())
    build(nc, *args)
    r = run_bass_kernel_spmd(nc, [arrays], core_ids=[0])
    return r.results[0]["out_x"]
```

```python
from contextlib import ExitStack

import concourse.bass as bass
import numpy as np
from concourse import mybir
from concourse.alu_op_type import AluOpType as ALU

F32 = mybir.dt.float32
BF16 = mybir.dt.bfloat16
I32 = mybir.dt.int32
ACT = mybir.ActivationFunctionType
AX = mybir.AxisListType

P = 128
D = 1024
TOK = 256
CTX = 256
KC = D // P
HEADS, HD = 16, 64
GRID_W, ROWS, WIN = 64, 4, 16
RPB_ROWS, RPB_COLS = 15, 31
E, TOPK = 32, 4
SLOTS = 64
MAX_EXTRA = (TOK * TOPK) // SLOTS - 1
NCOL = E + MAX_EXTRA + 1
EPS = 1e-6
NEG = -1.0e30
LIMIT, ALPHA = 7.0, 1.702
HALF = 512

RING = 12
ADA0, QK, VV, ADA1, ADA2, WO, EXP = 0, 8, 16, 20, 28, 36, 40
PER = 12
BIAS_SLOTS = 8


def build(nc, x, c, ctx_in, c_ctx, ada_w, ada_b, norm_g, w_qkv, w_o, rpb, w_router, b_router,
          w_up, b_up, w_down, b_down, out):
    with ExitStack() as st:
        def sb(name, shape, dt=F32):
            return st.enter_context(nc.sbuf_tensor(name, shape, dt))

        def sem(name):
            return st.enter_context(nc.semaphore(name))

        bank = [st.enter_context(nc.psum_tensor(f"bank{i}", [P, HALF], F32)) for i in range(8)]

        ring = sb("ring", [P, RING, 2048])
        tokens = sb("tokens", [P, 4, D])
        bias = tokens[:, :, :].rearrange("p a (b c) -> p (a b) c", c=512)
        hT_mem = sb("hT_mem", [P, KC * 512])
        hT = hT_mem[:, :].rearrange("p (k t) -> p k t", k=KC)
        oT = hT_mem[:, 0:2048].rearrange("p (k t) -> p k t", k=KC)
        acc = hT_mem[:, 2048:4096].rearrange("p (t d) -> p t d", t=2)
        kT_mem = sb("kT_mem", [P, KC * 512])
        kT = kT_mem[:, :].rearrange("p (k t) -> p k t", k=KC)
        x1 = kT_mem[:, 0:2048].rearrange("p (t d) -> p t d", t=2)
        h2T = kT_mem[:, 2048:4096].rearrange("p (k t) -> p k t", k=KC)
        q_mem = sb("q_mem", [P, KC * TOK])
        qT = q_mem[:, :].rearrange("p (k t) -> p k t", k=KC)
        h2 = q_mem[:, :].rearrange("p (t d) -> p t d", t=2)
        v_mem = sb("v_mem", [P, 4 * D])
        v = v_mem[:, :].rearrange("p (t d) -> p t d", t=4)
        xT = v_mem[:, 0:512].rearrange("p (j s) -> p j s", j=4)
        glu = v_mem[:, 512:1024]
        lin = v_mem[:, 1024:1536]
        sig = v_mem[:, 1536:2048]
        act = v_mem[:, 2048:2560]
        aT = v_mem[:, 2560:3072].rearrange("p (j s) -> p j s", j=4)
        y = v_mem[:, 3072:3584]
        combT = v_mem[:, 3584:3840].rearrange("p (t s) -> p t s", t=2)
        tmp = v_mem[:, 0:2048].rearrange("p (t d) -> p t d", t=2)
        junk = v_mem[:, 2048:3072]
        mod = [sb(f"mod{i}", [P, D]) for i in range(4)]
        gate1, shift2, scale2, gate2 = mod
        probs_mem = mod[2], mod[3]
        probs = [m[:, 512 * i:512 * i + 512] for m in probs_mem for i in range(2)]
        gain = sb("gain", [P, D])
        adab = sb("adab", [P, 3, HALF])
        rows = sb("rows", [P, HALF])
        pT_mem = sb("pT_mem", [P, 1024])
        probsT = hT_mem[:, 2048:4096].rearrange("p (u k t) -> p u k t", u=4, k=4)
        wtmp = pT_mem[:, 0:2 * GRID_W].rearrange("p (i c) -> p i c", i=2)
        grow = pT_mem[0:KC, 640:768]
        crow, csig = pT_mem[0:2 * KC, 768:896], pT_mem[0:2 * KC, 896:1024]
        small = pT_mem[:, 0:12 * E].rearrange("p (i e) -> p i e", e=E)
        pick = pT_mem[:, 384:512].rearrange("p (t s) -> p t s", t=2)
        gT = pT_mem[0:E, 768:768 + TOK]
        comb = pT_mem[:, 512:768].rearrange("p (t a s) -> p t a s", t=2, a=2)
        ident = sb("ident", [P, P])
        ones = sb("ones", [P, P])
        before = sb("before", [P, P])
        sel = sb("sel", [P, 2, P])
        pmod = sb("pmod", [P, 1])
        slot_no = sb("slot_no", [P, 2, SLOTS])
        qcol = sb("qcol", [P, 1])
        wmask = sb("wmask", [P, GRID_W])
        neghalf = sb("neghalf", [P, 1])
        condT = sb("condT", [P, KC, 32])
        gcol = sb("gcol", [P, KC])
        scol, hcol = sb("scol", [P, 4, 2, 2]), sb("hcol", [P, 4, 2, 2])
        ssq = sb("ssq", [P, 4])
        ssq2 = sb("ssq2", [P, 2, 2])
        ssq3 = sb("ssq3", [P, 2])
        ssq4 = sb("ssq4", [P, 2])
        ms = sb("ms", [P, 7, 2])
        rstd = sb("rstd", [P, 7, 2])
        nmax = sb("nmax", [P, 4])
        psum_p = sb("psum_p", [P, 4])
        rinv = sb("rinv", [P, 4])
        wr = sb("wr", [P, KC, E])
        br = sb("br", [P, E])
        bup = tokens[0:E, 0:2, :].rearrange("p a d -> p (a d)")
        xe = hT_mem[:, 0:HALF]
        bup_parts = tokens[:, 2, :].bitcast(BF16)[0:3 * E, :]
        bup_part = hT_mem[0:E, 2048:3072].bitcast(BF16)
        bdown = tokens[0:E, 3, :]
        rank_e, gate_e2 = small[:, 0:2, :], small[:, 4:6, :]
        rT, blocks, first = mod[1][0:E, 0:TOK], mod[1][0:E, 256:260], mod[1][0:E, 260:261]
        owner, base, place, inside = (mod[1][0:E, a:a + NCOL] for a in (320, 384, 448, 512))
        owner3 = mod[1][0:3 * E, 576:576 + NCOL]
        bsel = mod[1][0:3 * E, 640:640 + SLOTS // 2].bitcast(BF16)
        rank_col = sb("rank_col", [P, 2, NCOL])
        gate_col = sb("gate_col", [P, 2, NCOL])
        block_no = sb("block_no", [E, NCOL])
        whose_i = sb("whose_i", [1, NCOL], I32)
        ends_i = sb("ends_i", [1, E], I32)

        slot_in = [sem(f"slot_in{i}") for i in range(RING)]
        ring_free = sem("ring_free")
        in_g0, gcol_ready, cols_ready = sem("in_g0"), sem("gcol_ready"), sem("cols_ready")
        rowsT_done, mod_dve, mod_act = sem("rowsT_done"), sem("mod_dve"), sem("mod_act")
        in_c, in_adab, in_x, in_ctx = sem("in_c"), sem("in_adab"), sem("in_x"), sem("in_ctx")
        in_router, in_gain, in_res = sem("in_router"), sem("in_gain"), sem("in_res")
        in_bdown, in_bup, out_done = sem("in_bdown"), sem("in_bup"), sem("out_done")
        in_bias = [sem(f"in_bias{i}") for i in range(BIAS_SLOTS)]
        pool_step = sem("pool_step")
        consts = sem("consts")
        dve_step = sem("dve_step")
        adab_zero = sem("adab_zero")
        c_sig, c_silu, c_T, cond_ready = sem("c_sig"), sem("c_silu"), sem("c_T"), sem("cond_ready")
        rows_ready, bc_done = sem("rows_ready"), sem("bc_done")
        bc_dve, bc_act = sem("bc_dve"), sem("bc_act")
        ssq_ready, ms_ready, rstd_ready = sem("ssq_ready"), sem("ms_ready"), sem("rstd_ready")
        mod_ready, tr_done, tr_act = sem("mod_ready"), sem("tr_done"), sem("tr_act")
        proj_done, proj_act, proj_dve = sem("proj_done"), sem("proj_act"), sem("proj_dve")
        bias_ready, bias_used = sem("bias_ready"), sem("bias_used")
        s_done, max_ready, exp_ready = sem("s_done"), sem("max_ready"), sem("exp_ready")
        sum_inv, prob_ready, pT_done, pT_ready = sem("sum_inv"), sem("prob_ready"), sem("pT_done"), sem("pT_ready")
        o_done, o_ready = sem("o_done"), sem("o_ready")
        wo_done, x1_ready, h2_ready = sem("wo_done"), sem("x1_ready"), sem("h2_ready")
        h2T_done, h2T_ready, logit_done = sem("h2T_done"), sem("h2T_ready"), sem("logit_done")
        mx_used = sem("mx_used")
        exp_gate_in, exp_gate = sem("exp_gate_in"), sem("exp_gate")
        mask_ready, gates_ready, rank_done = sem("mask_ready"), sem("gates_ready"), sem("rank_done")
        gT_done, gT_ready = sem("gT_done"), sem("gT_ready")
        counts_done, blocks_ready, first_done = sem("counts_done"), sem("blocks_ready"), sem("first_done")
        owner_ready, rT_done, rT_ready, tables_done = sem("owner_ready"), sem("rT_done"), sem("rT_ready"), sem("tables_done")
        tables_ready, rank_ready, bsel_ready, bup_split = sem("tables_ready"), sem("rank_ready"), sem("bsel_ready"), sem("bup_split")
        xe_ready, xeT_done = sem("xe_ready"), sem("xeT_done")
        pick_ready, comb_ready = sem("pick_ready"), sem("comb_ready")
        gather_done, xT_ready, combT_done, combT_ready = sem("gather_done"), sem("xT_ready"), sem("combT_done"), sem("combT_ready")
        up_done, glu_ready, lin_ready = sem("up_done"), sem("glu_ready"), sem("lin_ready")
        sig_ready, pre_ready, act_ready = sem("sig_ready"), sem("pre_ready"), sem("act_ready")
        aT_low, aT_high, aT_dve, aT_act = sem("aT_low"), sem("aT_high"), sem("aT_dve"), sem("aT_act")
        y_ready = sem("y_ready")
        part_done, acc_done = sem("part_done"), sem("acc_done")
        fin_ready = sem("fin_ready")

        def uses_before(slot):
            return len([n for n in range(EXP) if n % RING == slot])

        def chunk_here(eng, n):
            eng.wait_ge(slot_in[n % RING], 16 * (n // RING + 1))

        def expert_chunk_here(eng, e, j):
            s = (EXP + j) % RING
            eng.wait_ge(slot_in[s], e * 16 + 16 * (uses_before(s) + 1))

        def proj_here(eng, i):
            if i == 15:
                eng.wait_ge(ring_free, VV)
            elif i == 23:
                eng.wait_ge(ring_free, ADA1)
            else:
                eng.wait_ge(proj_done, i + 1 - (i > 15))

        def by_row(t):
            return t.rearrange("p (r c) -> p r c", c=GRID_W)

        def backwards(t):
            return by_row(t)[:, :, ::-1]

        def wchunk(n):
            return ring[:, n % RING, :]

        def wpair(n, i):
            return ring[:, (n + i // 2) % RING, D * (i % 2):D * (i % 2) + D]

        def load_bias(eng, h):
            s = h % BIAS_SLOTS
            for r in range(ROWS):
                first = (h * RPB_ROWS + 7 - r) * RPB_COLS + 15 - (GRID_W - 1)
                src = bass.AP(rpb.tensor, first, [[1, GRID_W], [RPB_COLS, ROWS], [1, GRID_W]])
                half = 64 * (r % 2)
                dst = bias[half:half + 64, s, 256 * (r // 2):256 * (r // 2) + 256]
                eng.dma_start(dst.rearrange("p (i c) -> p i c", i=ROWS), src).then_inc(in_bias[s], 16)

        def number_of_blocks(eng):
            eng.wait_ge(tables_ready, 1)
            return eng.value_load(ends_i[0:1, E - 1:E], min_val=E, max_val=E + MAX_EXTRA)

        TR_BANK = [2 + i % 6 for i in range(8)]
        BC1 = [(0, 0), (0, 1), (0, 2), (0, 3)]
        UNITS = [(2 * p + j, t) for p in range(HEADS // 2) for t in range(2) for j in range(2)]
        BD_BANKS = (4, 2, 0, 1)
        MASK_AT = [9 + 2 * i for i in range(HEADS - BIAS_SLOTS)]
        ADA2_AT = 8

        block = st.enter_context(nc.Block())

        @block.sync
        def _(sp):
            ada_k = ada_w[0].rearrange("(k p) n -> k p n", p=P)
            qkv_k = w_qkv[0].rearrange("(k p) n -> k p n", p=P)
            v_2k = w_qkv[0].rearrange("(j k p) n -> j p k n", p=P, k=2)
            wo_2k = w_o[0].rearrange("(j k p) n -> j p k n", p=P, k=2)

            def source(n):
                if n < QK:
                    return ada_k[n - ADA0, :, 0:2048]
                if n < VV:
                    return qkv_k[n - QK, :, 0:2048]
                if n < ADA1:
                    return v_2k[n - VV, :, :, 2048:3072]
                if n < ADA2:
                    return ada_k[n - ADA1, :, 2048:4096]
                if n < WO:
                    return ada_k[n - ADA2, :, 4096:6144]
                return wo_2k[n - WO, :, :, :]

            def load(n):
                if n >= RING:
                    sp.wait_ge(ring_free, n - RING + 1)
                src = source(n)
                dst = wchunk(n)
                if len(src.shape) == 3:
                    dst = dst.rearrange("p (k n) -> p k n", k=2)
                sp.dma_start(dst, src).then_inc(slot_in[n % RING], 16)

            for n in range(ADA1):
                load(n)
            sp.wait_ge(tr_done, 8)
            for h in range(BIAS_SLOTS):
                load_bias(sp, h)
            for n in range(ADA1, EXP):
                load(n)

            up_k = w_up[0].rearrange("e (k p) n -> e k p n", p=P)
            down_2k = w_down[0].rearrange("e (j k p) n -> e j p k n", p=P, k=2)

            def expert(e, blocks_before):
                for j in range(PER):
                    sp.wait_ge(ring_free, blocks_before * PER + (EXP + j - RING + 1))
                    s = (EXP + j) % RING
                    if j < KC:
                        src = up_k[bass.ds(e, 1), j].rearrange("a p n -> (a p) n")
                        sp.dma_start(ring[:, s, :], src).then_inc(slot_in[s], 16)
                    else:
                        src = down_2k[bass.ds(e, 1), j - KC].rearrange("a p k n -> (a p) k n")
                        dst = ring[:, s, :].rearrange("p (k n) -> p k n", k=2)
                        sp.dma_start(dst, src).then_inc(slot_in[s], 16)

            expert(0, 0)
            sp.wait_ge(tables_ready, 1)
            with sp.Fori(1, E) as e:
                blocks_before = sp.value_load(ends_i[0:1, bass.ds(e - 1, 1)], min_val=1, max_val=E + MAX_EXTRA)
                expert(e, blocks_before)
            for t in range(2):
                sp.wait_ge(fin_ready, t + 1)
                sp.dma_start(out[0][P * t:P * t + P, :], tmp[:, t, :]).then_inc(out_done, 16)
            sp.wait_ge(out_done, 32)

        @block.gpsimd
        def _(pool):
            g = nc.gpsimd
            n = 0
            pool.dma_start(gain[:, :], norm_g[0][1:2, :].to_broadcast([P, D])).then_inc(in_gain, 16)
            g.memset(ones[:, :], 1.0).then_inc(pool_step, 1)
            g.memset(ident[:, :], 0.0).then_inc(pool_step, 1)
            g.memset(neghalf[:, :], -0.5).then_inc(consts, 1)
            g.iota(slot_no[:, :, :], [[0, 2], [1, SLOTS]], base=0, channel_multiplier=0,
                   allow_small_or_imprecise_dtypes=True).then_inc(consts, 1)
            pool.wait_ge(pool_step, 2)
            for j in range(4):
                pool.wait_ge(consts, 2 + j)
                g.iota(pmod[32 * j:32 * j + 32, :], [[0, 1]], base=0, channel_multiplier=1,
                       allow_small_or_imprecise_dtypes=True).then_inc(consts, 1)
            pool.wait_ge(consts, 6)
            g.iota(block_no[:, :], [[1, NCOL]], base=0, channel_multiplier=0,
                   allow_small_or_imprecise_dtypes=True).then_inc(consts, 1)
            pool.wait_ge(consts, 7)
            g.affine_select(out=ident[:, :], in_=ident[:, :], compare_op=ALU.not_equal, fill=1.0, base=0,
                            pattern=[[-1, P]], channel_multiplier=1).then_inc(consts, 1)
            g.affine_select(out=before[:, :], in_=ones[:, :], compare_op=ALU.is_gt, fill=0.0, base=0,
                            pattern=[[1, P]], channel_multiplier=-1).then_inc(consts, 1)

            def powers(k, cols):
                pool.wait_ge(ms_ready, k + 1)
                g.tensor_tensor(rstd[:, k, 0:cols], ms[:, k, 0:cols], neghalf[:, 0:1].to_broadcast([P, cols]),
                                ALU.pow).then_inc(rstd_ready, 1)

            powers(0, 2)
            powers(1, 2)

            pool.wait_ge(consts, 9)
            pool.wait_ge(rstd_ready, 2)
            for j in range(2):
                pool.wait_ge(pool_step, 2 + j)
                g.iota(qcol[64 * j:64 * j + 64, :], [[0, 1]], base=GRID_W - 1, channel_multiplier=-1,
                       allow_small_or_imprecise_dtypes=True).then_inc(pool_step, 1)
            pool.wait_ge(pool_step, 4)
            g.iota(wmask[:, :], [[1, GRID_W]], base=0, channel_multiplier=0,
                   allow_small_or_imprecise_dtypes=True).then_inc(pool_step, 1)
            pool.wait_ge(pool_step, 5)
            g.tensor_scalar(qcol[:, :], qcol[:, :], -float(WIN // 2), 0.0, ALU.add, ALU.max).then_inc(pool_step, 1)
            pool.wait_ge(pool_step, 6)
            g.tensor_scalar(qcol[:, :], qcol[:, :], float(GRID_W - WIN), 0.0, ALU.min, ALU.add).then_inc(pool_step, 1)
            pool.wait_ge(pool_step, 7)
            g.tensor_scalar(wmask[:, :], wmask[:, :], qcol[:, 0:1], None, ALU.subtract).then_inc(pool_step, 1)
            pool.wait_ge(pool_step, 8)
            g.tensor_scalar(wtmp[:, 0, :], wmask[:, :], 0.0, NEG, ALU.is_lt, ALU.mult).then_inc(pool_step, 1)
            g.tensor_scalar(wtmp[:, 1, :], wmask[:, :], float(WIN - 1), NEG, ALU.is_gt, ALU.mult).then_inc(pool_step, 1)
            pool.wait_ge(pool_step, 10)
            g.tensor_tensor(wmask[:, :], wtmp[:, 0, :], wtmp[:, 1, :], ALU.add).then_inc(pool_step, 1)
            pool.wait_ge(pool_step, 11)

            def gain_row(i):
                pool.wait_ge(bc_dve, 2 * i - 2)
                pool.dma_start(gain[:, :], norm_g[0][i:i + 1, :].to_broadcast([P, D])).then_inc(in_gain, 16)

            def mask_bias(h):
                s = h % BIAS_SLOTS
                pool.wait_ge(in_bias[s], 64 * (h // BIAS_SLOTS + 1))
                rows8 = bias[:, s, :].rearrange("p (i c) -> p i c", c=GRID_W)
                g.tensor_tensor(rows8, rows8, wmask[:, :].unsqueeze(1).to_broadcast([P, 8, GRID_W]),
                                ALU.add).then_inc(bias_ready, 1)

            for h in range(BIAS_SLOTS):
                mask_bias(h)
            gain_row(2)
            for u in range(len(UNITS)):
                pool.wait_ge(sum_inv, u + 1)
                g.tensor_scalar(probs[u % 4], probs[u % 4], rinv[:, u % 4:u % 4 + 1], 1.0, ALU.mult,
                                ALU.mult).then_inc(prob_ready, 1)
                if u in MASK_AT:
                    mask_bias(BIAS_SLOTS + MASK_AT.index(u))
            gain_row(3)
            for k in range(2, 6):
                powers(k, 1)
            powers(6, 2)

        @block.scalar
        def _(sc):
            s = nc.scalar
            sc.dma_start(crow[0:KC, :], c.rearrange("a (k p) -> (a k) p", p=P)).then_inc(in_c, 16)
            sc.dma_start(crow[KC:2 * KC, :], c_ctx.rearrange("(k p) -> k p", p=P)).then_inc(in_c, 16)
            sc.dma_start(grow, norm_g[0][0:1, :].rearrange("a (k p) -> (a k) p", p=P)).then_inc(in_g0, 16)
            x_t = x[0].rearrange("(t p) d -> p t d", p=P)
            sc.dma_start(tokens[:, 0:2, :], x_t).then_inc(in_x, 16)
            sc.dma_start(tokens[:, 2:4, :], ctx_in[0].rearrange("(t p) d -> p t d", p=P)).then_inc(in_ctx, 16)
            sc.wait_ge(adab_zero, 1)
            for r in range(2):
                sc.dma_start(adab[r:r + 97:32, :, :], ada_b[0].rearrange("(g j n) -> j g n", g=3, j=4)).then_inc(in_adab, 16)
            sc.dma_start(wr[:, :, :], w_router[0].rearrange("(k p) e -> p k e", p=P)).then_inc(in_router, 16)
            sc.dma_start(br[:, :], b_router[0:1, :].to_broadcast([P, E])).then_inc(in_router, 16)

            sc.wait_ge(in_c, 32)
            s.activation(csig, crow, ACT.Sigmoid).then_inc(c_sig, 1)
            sc.wait_ge(c_T, 1)
            sc.wait_ge(cond_ready, 1)
            s.activation(gcol[:, :], bank[1][:, 2 * KC:3 * KC], ACT.Copy).then_inc(gcol_ready, 1)
            s.activation(condT[:, :, 0:2], bank[1][:, 0:2 * KC].rearrange("p (r k) -> p k r", r=2),
                         ACT.Copy).then_inc(cond_ready, 1)
            for t in range(4):
                sc.wait_ge(in_x if t < 2 else in_ctx, 16)
                s.activation(kT_mem[:, D * t:D * t + D], tokens[:, t, :], ACT.Square,
                             accum_out=ssq[:, t:t + 1]).then_inc(ssq_ready, 1)
            for i in range(8):
                sc.wait_ge(tr_done, i + 1)
                t, k0 = i // 2, 4 * (i % 2)
                s.activation(hT[:, k0:k0 + 4, P * t:P * t + P], bank[TR_BANK[i]][:, :].rearrange("p (k t) -> p k t", k=4),
                             ACT.Copy).then_inc(tr_act, 1)
            sc.wait_ge(cols_ready, 4)
            sc.wait_ge(tr_act, 8)
            for part in range(2):
                for k in range(1, KC, 2):
                    h = hT[:, k, TOK * part:TOK * part + TOK]
                    s.activation(h, h, ACT.Identity, bias=hcol[:, k % 4, k // 4, part:part + 1],
                                 scale=scol[:, k % 4, k // 4, part:part + 1]).then_inc(mod_act, 1)
            for i in range(0, 24, 2):
                proj_here(sc, i)
                if i < 8:
                    s.activation(by_row(qT[:, i, :]), backwards(bank[i % 8][:, 0:TOK]), ACT.Copy, scale=HD ** -0.5).then_inc(proj_act, 1)
                elif i < 16:
                    s.activation(kT[:, i - 8, :], bank[i % 8][:, :], ACT.Copy).then_inc(proj_act, 1)
                else:
                    s.activation(v[:, (i - 16) // 2, 0:HALF], bank[i % 8][:, :], ACT.Copy).then_inc(proj_act, 1)

            def take_shift2():
                for i in range(2):
                    sc.wait_ge(bc_done, 2 + i + 1)
                    s.activation(shift2[:, HALF * i:HALF * i + HALF], bank[5 + i][:, :], ACT.Copy).then_inc(bc_act, 1)

            def softmax_exp(u):
                sc.wait_ge(max_ready, u + 1)
                if u >= 4:
                    sc.wait_ge(pT_done, u - 3)
                s.activation(probs[u % 4], bank[u % 3][:, :], ACT.Exp, bias=nmax[:, u % 4:u % 4 + 1],
                             accum_out=psum_p[:, u % 4:u % 4 + 1]).then_inc(exp_ready, 1)

            def take_probsT(u):
                sc.wait_ge(pT_done, u + 1)
                if u >= 4:
                    sc.wait_ge(o_done, u // 2 - 1)
                s.activation(probsT[:, u % 4, :, :], bank[3 + u % 2][:, :].rearrange("p (k t) -> p k t", k=4),
                             ACT.Copy).then_inc(pT_ready, 1)

            for u in range(len(UNITS)):
                softmax_exp(u)
                if u == 1:
                    take_shift2()
                if u >= 2:
                    take_probsT(u - 2)
                if u % 4 == 3 and u // 2 < HEADS - BIAS_SLOTS:
                    sc.wait_ge(bias_used, u + 1)
                    for h in UNITS[u - 1][0], UNITS[u][0]:
                        load_bias(sc, h + BIAS_SLOTS)
            take_probsT(len(UNITS) - 2)
            take_probsT(len(UNITS) - 1)
            def take_exp_gate(t):
                sc.wait_ge(exp_gate_in, t + 1)
                s.activation(small[:, 8 + t, :], small[:, t, :], ACT.Exp, bias=nmax[:, t:t + 1]).then_inc(exp_gate, 1)

            sc.wait_ge(s_done, len(UNITS))
            sc.dma_start(x1, x_t).then_inc(in_res, 16)
            sc.wait_ge(bias_used, len(UNITS))
            sc.dma_start(bup, b_up[0]).then_inc(in_bup, 16)
            sc.dma_start(bdown, b_down[0]).then_inc(in_bdown, 16)
            for t in range(2):
                if t == 0:
                    sc.wait_ge(wo_done, 1)
                else:
                    sc.wait_ge(ring_free, EXP)
                    sc.wait_ge(ssq_ready, 7)
                for i in range(2):
                    s.activation(junk[:, HALF * i:HALF * i + HALF], bank[4 + 2 * t + i][:, :], ACT.Square,
                                 accum_out=ssq2[:, t, i:i + 1]).then_inc(ssq_ready, 1)
                sc.wait_ge(x1_ready, t + 1)
                sc.wait_ge(ssq_ready, 6 + 3 * t)
                s.activation(junk, x1[:, t, :], ACT.Square, accum_out=ssq3[:, t:t + 1]).then_inc(ssq_ready, 1)
            for t in range(2):
                for i in range(2 * t, 2 * t + 2):
                    sc.wait_ge(h2T_done, i + 1)
                    k0 = 4 * (i % 2)
                    s.activation(h2T[:, k0:k0 + 4, P * t:P * t + P], bank[i][:, :].rearrange("p (k t) -> p k t", k=4),
                                 ACT.Copy).then_inc(h2T_ready, 1)
                if t == 1:
                    take_exp_gate(0)
            take_exp_gate(1)

            def take_xe(b):
                sc.wait_ge(gather_done, b + 1)
                s.activation(xe, bank[3][:, :], ACT.Copy).then_inc(xe_ready, 1)

            def take_xT(b):
                sc.wait_ge(xeT_done, b + 1)
                s.activation(xT, bank[3][:, :].rearrange("p (j s) -> p j s", j=4), ACT.Copy).then_inc(xT_ready, 1)

            sc.wait_ge(gT_done, 1)
            s.activation(gT, bank[7][0:E, 0:TOK], ACT.Copy).then_inc(gT_ready, 1)
            take_xe(0)
            sc.wait_ge(rT_done, 1)
            s.activation(rT, bank[7][0:E, 0:TOK], ACT.Copy).then_inc(rT_ready, 1)
            take_xT(0)
            for i in range(4):
                sc.wait_ge(part_done, i + 1)
                s.activation(acc[:, i // 2, HALF * (i % 2):HALF * (i % 2) + HALF], bank[BD_BANKS[i]][:, :],
                             ACT.Copy).then_inc(acc_done, 1)

            def block_step(b, is_first=False):
                sc.wait_ge(glu_ready, b + 1)
                s.activation(sig, glu, ACT.Sigmoid, scale=ALPHA).then_inc(sig_ready, 1)
                take_xe(b + 1)
                sc.wait_ge(combT_done, b + 1)
                if not is_first:
                    sc.wait_ge(part_done, b * 4 + 4)
                s.activation(combT, bank[4][:, 0:TOK].rearrange("p (t s) -> p t s", t=2), ACT.Copy).then_inc(combT_ready, 1)
                sc.wait_ge(aT_high, b + 1)
                s.activation(aT[:, 2:4, :], bank[4][:, 0:TOK].rearrange("p (j s) -> p j s", j=2),
                             ACT.Copy).then_inc(aT_act, 1)
                take_xT(b + 1)
                sc.wait_ge(ring_free, b * PER + (EXP + PER))
                s.activation(y, bank[2][:, :], ACT.Copy).then_inc(y_ready, 1)

            block_step(0, is_first=True)
            last_block = number_of_blocks(sc)
            with sc.Fori(1, last_block) as b:
                block_step(b)
            sc.wait_ge(acc_done, last_block * 4 + 4)
            for t in range(2):
                sc.wait_ge(ssq_ready, 10 + t)
                s.activation(junk, acc[:, t, :], ACT.Square,
                             accum_out=ssq4[:, t:t + 1]).then_inc(ssq_ready, 1)

        @block.vector
        def _(ve):
            d = nc.vector
            steps = [0]

            def step(ins):
                ins.then_inc(dve_step, 1)
                steps[0] += 1
                ve.wait_ge(dve_step, steps[0])

            d.memset(adab[:, :, :], 0.0).then_inc(adab_zero, 1)
            d.memset(condT[:, :, :], 0.0).then_inc(cond_ready, 1)
            ve.wait_ge(c_sig, 1)
            d.tensor_tensor(csig, csig, crow, ALU.mult).then_inc(c_silu, 1)
            ve.wait_ge(pool_step, 2)
            ve.wait_ge(consts, 9)
            d.tensor_scalar(sel[:, 0, :], ones[:, :], 1.0, pmod[:, 0:1], ALU.subtract, ALU.is_equal)
            step(d.tensor_scalar(sel[:, 1, :], ones[:, :], pmod[:, 0:1], None, ALU.is_equal))

            def mean_squares(k, src, cols):
                d.tensor_scalar(ms[:, k, 0:cols], src, 1.0 / D, EPS, ALU.mult, ALU.add).then_inc(ms_ready, 1)

            for part in range(2):
                ve.wait_ge(ssq_ready, 2 * part + 2)
                mean_squares(part, ssq[:, 2 * part:2 * part + 2], 2)
                ve.wait_ge(rstd_ready, part + 1)
                for t in range(2 * part, 2 * part + 2):
                    d.tensor_scalar(tokens[:, t, :], tokens[:, t, :], rstd[:, part, t % 2:t % 2 + 1], None,
                                    ALU.mult).then_inc(mod_ready, 1)

            def take_rows(g):
                ve.wait_ge(ring_free, (ADA0, ADA1, ADA2)[g] + KC)
                if g == 0:
                    ve.wait_ge(in_adab, 32)
                else:
                    ve.wait_ge(rowsT_done if g == 1 else bc_done, (1, 4)[g - 1])
                b = (0, 7, 7)[g]
                d.tensor_tensor(rows[:, :], bank[b][:, :], adab[:, g, :], ALU.add).then_inc(rows_ready, 1)

            take_rows(0)
            ve.wait_ge(gcol_ready, 1)
            ve.wait_ge(rowsT_done, 1)
            cols = bank[1][:, :].rearrange("p (m j s) -> p m j s", m=4, j=4)
            gains = gcol[:, :].rearrange("p (j m) -> p m j", m=4)
            for part in range(2):
                d.scalar_tensor_tensor(scol[:, :, :, part], cols[:, :, 2:4, part], 1.0, gains, ALU.add, ALU.mult).then_inc(cols_ready, 1)
                d.tensor_copy(hcol[:, :, :, part], cols[:, :, 0:2, part]).then_inc(cols_ready, 1)
            ve.wait_ge(cols_ready, 4)
            ve.wait_ge(tr_act, 8)
            for part in range(2):
                for k in range(0, KC, 2):
                    h = hT[:, k, TOK * part:TOK * part + TOK]
                    d.tensor_scalar(h, h, scol[:, k % 4, k // 4, part:part + 1], hcol[:, k % 4, k // 4, part:part + 1],
                                    ALU.mult, ALU.add).then_inc(mod_dve, 1)
            for i in range(1, 24, 2):
                proj_here(ve, i)
                if i < 8:
                    d.tensor_scalar(by_row(qT[:, i, :]), backwards(bank[i % 8][:, 0:TOK]), HD ** -0.5, None, ALU.mult).then_inc(proj_dve, 1)
                elif i < 16:
                    d.tensor_copy(kT[:, i - 8, :], bank[i % 8][:, :]).then_inc(proj_dve, 1)
                else:
                    d.tensor_copy(v[:, (i - 16) // 2, HALF:D], bank[i % 8][:, :]).then_inc(proj_dve, 1)

            def make_gate1():
                ve.wait_ge(in_gain, 16)
                for i in range(2):
                    ve.wait_ge(bc_done, i + 1)
                    h = slice(HALF * i, HALF * i + HALF)
                    d.tensor_tensor(gate1[:, h], bank[3 + i][:, :], gain[:, h], ALU.mult).then_inc(bc_dve, 1)

            def scores(u):
                h, t = UNITS[u]
                ve.wait_ge(s_done, u + 1)
                if t == 0:
                    ve.wait_ge(bias_ready, h + 1)
                sl = bank[u % 3][:, 0:256]
                d.tensor_tensor(sl, sl, bias[:, h % BIAS_SLOTS, 256 * t:256 * t + 256], ALU.add).then_inc(bias_used, 1)
                ve.wait_ge(bias_used, u + 1)
                if u >= 4:
                    ve.wait_ge(exp_ready, u - 3)
                d.tensor_reduce(nmax[:, u % 4:u % 4 + 1], bank[u % 3][:, :], AX.X, ALU.max, negate=True).then_inc(max_ready, 1)

            def invert(u):
                ve.wait_ge(exp_ready, u + 1)
                if u >= 4:
                    ve.wait_ge(prob_ready, u - 3)
                d.reciprocal(rinv[:, u % 4:u % 4 + 1], psum_p[:, u % 4:u % 4 + 1]).then_inc(sum_inv, 1)

            def take_o(p):
                ve.wait_ge(o_done, 2 * p + 2)
                d.tensor_copy(by_row(oT[:, p, :]), backwards(bank[5 + p % 2][:, 0:TOK])).then_inc(o_ready, 1)

            for u in range(len(UNITS)):
                scores(u)
                if u >= 1:
                    invert(u - 1)
                if u >= 7 and u % 4 == 3:
                    take_o((u - 7) // 4)
                if u == 1:
                    take_rows(1)
                    make_gate1()
                if u == ADA2_AT + 1:
                    take_rows(2)
            invert(len(UNITS) - 1)
            take_o(HEADS // 2 - 1)
            ve.wait_ge(in_gain, 32)
            for i in range(2):
                ve.wait_ge(bc_done, 4 + i + 1)
                h = slice(HALF * i, HALF * i + HALF)
                d.scalar_tensor_tensor(scale2[:, h], bank[i][:, :], 1.0, gain[:, h], ALU.add, ALU.mult).then_inc(bc_dve, 1)
            ve.wait_ge(in_bup, 16)
            step(d.tensor_copy(bup_parts[0:E, :], bup))
            step(d.tensor_tensor(bup, bup, bup_parts[0:E, :], ALU.subtract))
            step(d.tensor_copy(bup_part, bup))
            step(d.tensor_tensor(bup, bup, bup_part, ALU.subtract))
            d.tensor_copy(bup_parts[E:2 * E, :], bup_part)
            d.tensor_copy(bup_parts[2 * E:3 * E, :], bup).then_inc(bup_split, 1)
            ve.wait_ge(in_gain, 48)
            for i in range(2):
                ve.wait_ge(bc_done, 6 + i + 1)
                h = slice(HALF * i, HALF * i + HALF)
                d.tensor_tensor(gate2[:, h], bank[2 + i][:, :], gain[:, h], ALU.mult).then_inc(bc_dve, 1)
            ve.wait_ge(in_res, 16)
            ve.wait_ge(bc_dve, 6)
            for t in range(2):
                for i in range(2):
                    ve.wait_ge(ssq_ready, 5 + 3 * t + i)
                    h = slice(HALF * i, HALF * i + HALF)
                    d.tensor_tensor(tmp[:, t, h], bank[4 + 2 * t + i][:, :], gate1[:, h], ALU.mult).then_inc(mx_used, 1)
                step(d.tensor_tensor(ssq2[:, t, 0:1], ssq2[:, t, 0:1], ssq2[:, t, 1:2], ALU.add))
                mean_squares(2 + 2 * t, ssq2[:, t, 0:1], 1)
                ve.wait_ge(mx_used, 2 * t + 2)
                ve.wait_ge(rstd_ready, 3 + 2 * t)
                d.scalar_tensor_tensor(x1[:, t, :], tmp[:, t, :], rstd[:, 2 + 2 * t, 0:1], x1[:, t, :],
                                       ALU.mult, ALU.add).then_inc(x1_ready, 1)
                ve.wait_ge(x1_ready, t + 1)
                step(d.tensor_tensor(h2[:, t, :], x1[:, t, :], scale2[:, :], ALU.mult))
                ve.wait_ge(ssq_ready, 7 + 3 * t)
                mean_squares(3 + 2 * t, ssq3[:, t:t + 1], 1)
                ve.wait_ge(rstd_ready, 4 + 2 * t)
                d.scalar_tensor_tensor(h2[:, t, :], h2[:, t, :], rstd[:, 3 + 2 * t, 0:1], shift2[:, :],
                                       ALU.mult, ALU.add).then_inc(h2_ready, 1)

            logit, top, over, tie, gate_e, mask = (small[:, 2 * i:2 * i + 2, :] for i in range(6))
            ve.wait_ge(in_router, 32)
            for t in range(2):
                ve.wait_ge(logit_done, t + 1)
                step(d.tensor_tensor(logit[:, t, :], bank[4 + t][:, 0:E], br[:, :], ALU.add))
                step(d.max(top[:, t, 0:8], logit[:, t, :]))
                d.tensor_scalar(nmax[:, t:t + 1], top[:, t, 0:1], -1.0, None, ALU.mult).then_inc(exp_gate_in, 1)
                d.tensor_scalar(over[:, t, :], logit[:, t, :], top[:, t, TOPK - 1:TOPK], None, ALU.is_gt)
                step(d.tensor_scalar(tie[:, t, :], logit[:, t, :], top[:, t, TOPK - 1:TOPK], None, ALU.is_equal))
                step(d.tensor_reduce(top[:, t, 8:9], over[:, t, :], AX.X, ALU.add, negate=True))
                d.tensor_scalar(top[:, t, 9:10], top[:, t, 8:9], float(TOPK), None, ALU.add)
                step(d.tensor_tensor_scan(mask[:, t, :], ones[:, 0:E], tie[:, t, :], 0.0, ALU.mult, ALU.add))
                step(d.tensor_scalar(mask[:, t, :], mask[:, t, :], top[:, t, 9:10], None, ALU.is_le))
                step(d.tensor_tensor(mask[:, t, :], mask[:, t, :], tie[:, t, :], ALU.mult))
                d.tensor_tensor(mask[:, t, :], mask[:, t, :], over[:, t, :], ALU.add).then_inc(mask_ready, 1)
                ve.wait_ge(mask_ready, t + 1)
                ve.wait_ge(exp_gate, t + 1)
                step(d.tensor_tensor(gate_e[:, t, :], gate_e[:, t, :], mask[:, t, :], ALU.mult))
                step(d.tensor_reduce(top[:, t, 10:11], gate_e[:, t, :], AX.X, ALU.add))
                step(d.reciprocal(top[:, t, 11:12], top[:, t, 10:11]))
                d.tensor_scalar(gate_e2[:, t, :], gate_e[:, t, :], top[:, t, 11:12], None, ALU.mult).then_inc(gates_ready, 1)
            ve.wait_ge(gates_ready, 2)
            ve.wait_ge(rank_done, 1)
            for t in range(2):
                step(d.scalar_tensor_tensor(rank_e[:, t, :], bank[6][:, E * t:E * t + E], 1.0, mask[:, t, :], ALU.add, ALU.mult))
                d.tensor_scalar(rank_e[:, t, :], rank_e[:, t, :], -1.0, None, ALU.add).then_inc(rank_ready, 1)
            ve.wait_ge(rank_ready, 2)

            def make_pick(ranks, b):
                for t in range(2):
                    ins = d.tensor_scalar(pick[:, t, :], slot_no[:, 0, :], ranks[:, t, bass.ds(b, 1)], None, ALU.is_equal)
                ins.then_inc(pick_ready, 1)

            def make_comb(ranks, gates, b):
                for t in range(2):
                    ins = d.tensor_scalar(comb[:, t, :, :], slot_no[:, :, :], ranks[:, t, bass.ds(b, 1)],
                                          gates[:, t, bass.ds(b, 1)], ALU.is_equal, ALU.mult)
                ins.then_inc(comb_ready, 1)

            def make_bsel(b):
                d.tensor_copy(bsel, owner3[:, bass.ds(b, 1)].to_broadcast([3 * E, SLOTS])).then_inc(bsel_ready, 1)

            make_pick(rank_e, 0)
            ve.wait_ge(counts_done, 1)
            step(d.tensor_copy(blocks[:, 3:4], bank[6][0:E, 0:1]))
            step(d.tensor_scalar(blocks[:, 0:1], blocks[:, 3:4], float(SLOTS), 1.0, ALU.is_gt, ALU.add))
            step(d.tensor_scalar(blocks[:, 1:2], blocks[:, 3:4], float(2 * SLOTS), blocks[:, 0:1], ALU.is_gt, ALU.add))
            d.tensor_scalar(blocks[:, 2:3], blocks[:, 3:4], float(3 * SLOTS), blocks[:, 1:2], ALU.is_gt, ALU.add).then_inc(blocks_ready, 1)
            make_comb(rank_e, gate_e2, 0)
            ve.wait_ge(first_done, 1)
            ve.wait_ge(blocks_ready, 1)
            step(d.tensor_copy(first, bank[6][0:E, 0:1]))
            step(d.tensor_scalar(place, block_no[:, :], first, None, ALU.subtract))
            step(d.tensor_scalar(inside, place, blocks[:, 2:3], None, ALU.is_lt))
            step(d.scalar_tensor_tensor(owner, place, 0.0, inside, ALU.is_ge, ALU.mult))
            d.scalar_tensor_tensor(base, place, -float(SLOTS), owner, ALU.mult, ALU.mult).then_inc(owner_ready, 1)
            for i in range(3):
                ins = d.tensor_copy(owner3[E * i:E * i + E, :], owner)
            step(ins)
            make_bsel(0)
            ve.wait_ge(tables_done, 1)
            d.tensor_copy(whose_i[:, :], bank[6][0:1, 64:64 + NCOL])
            d.tensor_copy(ends_i[:, :], bank[6][0:1, 128:128 + E])
            d.tensor_copy(rank_col[:, :, :], bank[5][:, 0:2 * NCOL].rearrange("p (t b) -> p t b", t=2))
            ins = d.tensor_copy(gate_col[:, :, :], bank[5][:, 2 * NCOL:4 * NCOL].rearrange("p (t b) -> p t b", t=2))
            ins.then_inc(tables_ready, 1)
            ve.wait_ge(tables_ready, 1)

            def add_part(t, b):
                ve.wait_ge(part_done, b * 4 + (2 * t + 2))
                for n in range(2):
                    dst = acc[:, t, HALF * n:HALF * n + HALF]
                    d.tensor_tensor(dst, dst, bank[6 + n][:, :], ALU.add).then_inc(acc_done, 1)

            def block_step(b, is_first=False):
                ve.wait_ge(gather_done, b + 1)
                make_pick(rank_col, b + 1)
                ve.wait_ge(up_done, b + 1)
                d.tensor_scalar(glu, bank[0][:, :], LIMIT, None, ALU.min).then_inc(glu_ready, 1)
                d.tensor_scalar(lin, bank[1][:, :], LIMIT, -LIMIT, ALU.min, ALU.max).then_inc(lin_ready, 1)
                ve.wait_ge(glu_ready, b + 1)
                ve.wait_ge(lin_ready, b + 1)
                d.scalar_tensor_tensor(act, lin, 1.0, glu, ALU.add, ALU.mult).then_inc(pre_ready, 1)
                if not is_first:
                    ve.wait_ge(acc_done, b * 4)
                    add_part(0, b)
                ve.wait_ge(pre_ready, b + 1)
                ve.wait_ge(sig_ready, b + 1)
                d.tensor_tensor(act, act, sig, ALU.mult).then_inc(act_ready, 1)
                make_bsel(b + 1)
                ve.wait_ge(aT_low, b + 1)
                d.tensor_copy(aT[:, 0:2, :], bank[5][:, 0:TOK].rearrange("p (j s) -> p j s", j=2)).then_inc(aT_dve, 1)
                if not is_first:
                    add_part(1, b)
                ve.wait_ge(combT_done, b + 1)
                make_comb(rank_col, gate_col, b + 1)

            block_step(0, is_first=True)
            last_block = number_of_blocks(ve)
            with ve.Fori(1, last_block) as b:
                block_step(b)
            ve.wait_ge(acc_done, last_block * 4)
            add_part(0, last_block)
            add_part(1, last_block)
            ve.wait_ge(acc_done, last_block * 4 + 4)
            for t in range(2):
                ins = d.tensor_tensor(tmp[:, t, :], acc[:, t, :], gate2[:, :], ALU.mult)
            step(ins)
            ve.wait_ge(ssq_ready, 12)
            mean_squares(6, ssq4[:, :], 2)
            ve.wait_ge(rstd_ready, 7)
            for t in range(2):
                d.scalar_tensor_tensor(tmp[:, t, :], tmp[:, t, :], rstd[:, 6, t:t + 1], x1[:, t, :],
                                       ALU.mult, ALU.add).then_inc(fin_ready, 1)

        @block.tensor
        def _(pe):
            mm, tr = nc.tensor.matmul, nc.tensor.transpose

            pe.wait_ge(consts, 9)
            pe.wait_ge(c_silu, 1)
            pe.wait_ge(in_g0, 16)
            tr(bank[1][:, 2 * KC:3 * KC], grow, ident[0:KC, 0:KC])
            tr(bank[1][:, 0:2 * KC], csig, ident[0:2 * KC, 0:2 * KC]).then_inc(c_T, 1)
            pe.wait_ge(cond_ready, 2)

            def transpose_tokens(i):
                t, k0 = i // 2, 4 * (i % 2)
                pe.wait_ge(mod_ready, t + 1)
                if i >= 6:
                    pe.wait_ge(tr_act, i - 5)
                for j in range(4):
                    last = tr(bank[TR_BANK[i]][:, P * j:P * j + P], tokens[:, t, P * (k0 + j):P * (k0 + j) + P], ident[:, :])
                last.then_inc(tr_done, 1)

            def ada(g, b):
                for k in range(KC):
                    n = (ADA0, ADA1, ADA2)[g] + k
                    chunk_here(pe, n)
                    for j in range(4):
                        last = mm(bank[b][32 * j:32 * j + 32, :], condT[:, k, :], wchunk(n)[:, HALF * j:HALF * j + HALF],
                                  start=k == 0, stop=k == KC - 1)
                    last.then_inc(ring_free, 1)
                    if g == 0:
                        for i in {3: (0, 1), 4: (2, 3), 6: (4, 5), 7: (6, 7)}.get(k, ()):
                            transpose_tokens(i)

            def broadcast(jobs, banks):
                for (r, j), b in zip(jobs, banks):
                    mm(bank[b][:, :], sel[32 * j:32 * j + 32, r, :], rows[32 * j:32 * j + 32, :],
                       start=True, stop=True).then_inc(bc_done, 1)

            ada(0, 0)
            pe.wait_ge(rows_ready, 1)
            for m in range(4):
                last = tr(bank[1][:, P * m:P * m + P], rows[:, P * m:P * m + P], ident[:, :])
            last.then_inc(rowsT_done, 1)
            for what in range(3):
                for k in range(KC):
                    if what == 0:
                        chunk_here(pe, QK + k)
                    elif what == 2 and k % 2 == 0:
                        chunk_here(pe, VV + k // 2)
                    if what < 2:
                        pe.wait_ge(mod_act if k % 2 else mod_dve, 4 * what + k // 2 + 1)
                    for i in range(8):
                        n = 8 * what + i
                        if what > 0 and k == 0:
                            pe.wait_ge(proj_act if n % 2 == 0 else proj_dve, (n - 8) // 2 + 1)
                        if what == 0:
                            last = mm(bank[i][:, 0:TOK], wchunk(QK + k)[:, P * i:P * i + P], hT[:, k, 0:TOK],
                                      start=k == 0, stop=k == KC - 1)
                        elif what == 1:
                            last = mm(bank[i][:, :], wchunk(QK + k)[:, P * n:P * n + P], hT[:, k, :],
                                      start=k == 0, stop=k == KC - 1)
                        else:
                            t, j = i // 2, i % 2
                            last = mm(bank[i][:, :], hT[:, k, P * t:P * t + P], wpair(VV, k)[:, HALF * j:HALF * j + HALF],
                                      start=k == 0, stop=k == KC - 1)
                        if k == KC - 1 and n not in (15, 23):
                            last.then_inc(proj_done, 1)
                    if what == 1 or (what == 2 and k % 2 == 1):
                        last.then_inc(ring_free, 1)

            def score(u):
                h, t = UNITS[u]
                p0 = HD * (h % 2)
                if u >= 3:
                    pe.wait_ge(exp_ready, u - 2)
                mm(bank[u % 3][:, :], qT[p0:p0 + HD, h // 2, P * t:P * t + P], kT[p0:p0 + HD, h // 2, :],
                   start=True, stop=True).then_inc(s_done, 1)

            def transpose_probs(u):
                pe.wait_ge(prob_ready, u + 1)
                if u >= 2:
                    pe.wait_ge(pT_ready, u - 1)
                for kc in range(4):
                    last = tr(bank[3 + u % 2][:, P * kc:P * kc + P], probs[u % 4][:, P * kc:P * kc + P], ident[:, :])
                last.then_inc(pT_done, 1)

            def mix(m):
                p, t = m // 2, m % 2
                pe.wait_ge(pT_ready, 2 * m + 2)
                if p >= 2:
                    pe.wait_ge(o_ready, p - 1)
                for kc in range(4):
                    for j in range(2):
                        h = 2 * p + j
                        last = mm(bank[5 + p % 2][HD * j:HD * j + HD, P * t:P * t + P], v[:, kc, HD * h:HD * h + HD],
                                  probsT[:, (2 * m + j) % 4, kc, :], start=kc == 0, stop=kc == 3)
                last.then_inc(o_done, 1)

            pe.wait_ge(proj_act, 12)
            pe.wait_ge(proj_dve, 12)
            score(0)
            score(1)
            ada(1, 7)
            for u in range(len(UNITS)):
                if u == ADA2_AT:
                    ada(2, 7)
                if u + 2 < len(UNITS):
                    score(u + 2)
                if u == 0:
                    pe.wait_ge(rows_ready, 2)
                    pe.wait_ge(dve_step, 1)
                    broadcast(BC1, range(3, 7))
                if u == 1:
                    pe.wait_ge(bc_dve, 2)
                    pe.wait_ge(bc_act, 2)
                if u >= 1:
                    transpose_probs(u - 1)
                if u >= 3 and u % 2 == 1:
                    mix((u - 3) // 2)
            transpose_probs(len(UNITS) - 1)
            mix(len(UNITS) // 2 - 1)

            pe.wait_ge(rows_ready, 3)
            broadcast(BC1, range(4))
            pe.wait_ge(o_ready, HEADS // 2)
            for t in range(2):
                for i in range(2):
                    for k in range(KC):
                        if t == 0 and i == 0 and k % 2 == 0:
                            chunk_here(pe, WO + k // 2)
                        last = mm(bank[4 + 2 * t + i][:, :], oT[:, k, P * t:P * t + P],
                                  wpair(WO, k)[:, HALF * i:HALF * i + HALF], start=k == 0, stop=k == KC - 1)
                        if t == 1 and i == 1 and k % 2 == 1:
                            last.then_inc(ring_free, 1)
                if t == 0:
                    last.then_inc(wo_done, 1)
            pe.wait_ge(bc_dve, 6)
            pe.wait_ge(in_router, 32)
            for t in range(2):
                pe.wait_ge(h2_ready, t + 1)
                for i in range(2 * t, 2 * t + 2):
                    for j in range(4):
                        k = 4 * (i % 2) + j
                        last = tr(bank[i][:, P * j:P * j + P], h2[:, t, P * k:P * k + P], ident[:, :])
                    last.then_inc(h2T_done, 1)
                pe.wait_ge(mx_used, 2 * t + 2)
                for k in range(KC):
                    if k % 4 == 0:
                        pe.wait_ge(h2T_ready, 2 * t + k // 4 + 1)
                    last = mm(bank[4 + t][:, 0:E], h2T[:, k, P * t:P * t + P], wr[:, k, :], start=k == 0, stop=k == KC - 1)
                last.then_inc(logit_done, 1)
            pe.wait_ge(mask_ready, 2)
            mask = small[:, 10:12, :]
            mm(bank[6][:, 0:E], before[:, :], mask[:, 0, :], start=True, stop=True)
            mm(bank[6][:, E:2 * E], before[:, :], mask[:, 1, :], start=True, stop=False)
            mm(bank[6][:, E:2 * E], ones[:, :], mask[:, 0, :], start=False, stop=True)
            mm(bank[6][:, 2 * E:3 * E], ones[:, :], mask[:, 0, :], start=True, stop=False)
            mm(bank[6][:, 2 * E:3 * E], ones[:, :], mask[:, 1, :], start=False, stop=True).then_inc(rank_done, 1)
            pe.wait_ge(gates_ready, 2)
            for t in range(2):
                last = tr(bank[7][0:E, P * t:P * t + P], gate_e2[:, t, :], ident[:, :])
            last.then_inc(gT_done, 1)

            def gather(b):
                pe.wait_ge(pick_ready, b + 1)
                for t in range(2):
                    for n in range(2):
                        last = mm(bank[3][64 * n:64 * n + 64, :], pick[:, t, :], h2[:, t, HALF * n:HALF * n + HALF],
                                  start=t == 0, stop=t == 1)
                last.then_inc(gather_done, 1)

            def transpose_xe(b):
                pe.wait_ge(xe_ready, b + 1)
                for j in range(4):
                    last = tr(bank[3][:, P * j:P * j + P], xe[:, P * j:P * j + P], ident[:, :])
                last.then_inc(xeT_done, 1)

            gather(0)
            for t in range(2):
                last = mm(bank[6][0:E, 0:1], mask[:, t, :], ones[:, 0:1], start=t == 0, stop=t == 1)
            last.then_inc(counts_done, 1)
            pe.wait_ge(gT_ready, 1)
            pe.wait_ge(in_bdown, 16)
            for i in range(4):
                t, n = i // 2, i % 2
                mm(bank[BD_BANKS[i]][:, :], gT[:, P * t:P * t + P], bdown[:, HALF * n:HALF * n + HALF],
                   start=True, stop=True).then_inc(part_done, 1)
            pe.wait_ge(rank_ready, 2)
            for t in range(2):
                last = tr(bank[7][0:E, P * t:P * t + P], rank_e[:, t, :], ident[:, :])
            last.then_inc(rT_done, 1)
            transpose_xe(0)
            pe.wait_ge(blocks_ready, 1)
            mm(bank[6][0:E, 0:1], before[0:E, 0:E], blocks[:, 2:3], start=True, stop=True).then_inc(first_done, 1)
            pe.wait_ge(owner_ready, 1)
            pe.wait_ge(rT_ready, 1)
            mm(bank[6][0:1, 64:64 + NCOL], pmod[0:E, 0:1], owner, start=True, stop=True)
            mm(bank[6][0:1, 128:128 + E], blocks[:, 2:3], before[0:E, 0:E], start=True, stop=False)
            mm(bank[6][0:1, 128:128 + E], blocks[:, 2:3], ident[0:E, 0:E], start=False, stop=True)
            for t in range(2):
                mm(bank[5][:, NCOL * t:NCOL * t + NCOL], rT[:, P * t:P * t + P], owner, start=True, stop=False)
                mm(bank[5][:, NCOL * t:NCOL * t + NCOL], ones[0:E, :], base, start=False, stop=True)
            for t in range(2):
                last = mm(bank[5][:, NCOL * (2 + t):NCOL * (3 + t)], gT[:, P * t:P * t + P], owner, start=True, stop=True)
            last.then_inc(tables_done, 1)
            pe.wait_ge(acc_done, 4)

            def combine(t, b):
                pe.wait_ge(acc_done, b * 4 + 2 * t)
                for n in range(2):
                    mm(bank[6 + n][:, :], combT[64 * n:64 * n + 64, t, :], y[64 * n:64 * n + 64, :],
                       start=True, stop=True).then_inc(part_done, 1)

            def block_step(b, e, is_first=False):
                pe.wait_ge(xT_ready, b + 1)
                for k in range(KC):
                    expert_chunk_here(pe, e, k)
                    w = ring[:, (EXP + k) % RING, :]
                    for half in range(2):
                        for n in range(2):
                            c0 = D * half + HALF * n
                            last = mm(bank[half][64 * n:64 * n + 64, :], xT[:, k % 4, 64 * (k // 4):64 * (k // 4) + 64],
                                      w[:, c0:c0 + HALF], start=k == 0, stop=False)
                    last.then_inc(ring_free, 1)
                pe.wait_ge(bsel_ready, b + 1)
                for half in range(2):
                    for n in range(2):
                        c0 = D * half + HALF * n
                        last = mm(bank[half][64 * n:64 * n + 64, :], bsel, bup_parts[:, c0:c0 + HALF],
                                  start=False, stop=True)
                last.then_inc(up_done, 1)
                if not is_first:
                    pe.wait_ge(y_ready, b)
                    pe.wait_ge(combT_ready, b)
                    combine(0, b)
                pe.wait_ge(comb_ready, b + 1)
                for t in range(2):
                    last = tr(bank[4][:, P * t:P * t + P], comb[:, t, :, :].rearrange("p a s -> p (a s)"), ident[:, :])
                last.then_inc(combT_done, 1)
                gather(b + 1)
                if not is_first:
                    combine(1, b)
                pe.wait_ge(act_ready, b + 1)
                for j in range(2):
                    last = tr(bank[5][:, P * j:P * j + P], act[:, P * j:P * j + P], ident[:, :])
                last.then_inc(aT_low, 1)
                pe.wait_ge(combT_ready, b + 1)
                for j in range(2):
                    last = tr(bank[4][:, P * j:P * j + P], act[:, P * (2 + j):P * (2 + j) + P], ident[:, :])
                last.then_inc(aT_high, 1)
                transpose_xe(b + 1)
                pe.wait_ge(aT_dve, b + 1)
                pe.wait_ge(aT_act, b + 1)
                for k in range(KC):
                    if k % 2 == 0:
                        expert_chunk_here(pe, e, KC + k // 2)
                    w = ring[:, (EXP + KC + k // 2) % RING, D * (k % 2):D * (k % 2) + D]
                    half, j = k // 4, k % 4
                    for n in range(2):
                        last = mm(bank[2][64 * n:64 * n + 64, :], aT[:, j, 64 * half:64 * half + 64],
                                  w[:, HALF * n:HALF * n + HALF], start=k == 0, stop=k == KC - 1)
                    if k % 2 == 1:
                        last.then_inc(ring_free, 1)

            pe.wait_ge(bup_split, 1)
            block_step(0, 0, is_first=True)
            last_block = number_of_blocks(pe)
            with pe.Fori(1, last_block) as b:
                e = pe.value_load(whose_i[0:1, bass.ds(b, 1)], min_val=0, max_val=E - 1)
                block_step(b, e)
            pe.wait_ge(y_ready, last_block)
            pe.wait_ge(combT_ready, last_block)
            combine(0, last_block)
            combine(1, last_block)


_INS = ["x", "c", "ctx", "c_ctx", "ada_w", "ada_b", "norm_g", "na_w_qkv", "na_w_o", "na_rpb", "moe_w_router",
        "moe_b_router", "moe_w_up", "moe_b_up", "moe_w_down", "moe_b_down"]


def kernel(**inputs):
    import concourse.bacc as bacc
    from concourse.bass_utils import run_bass_kernel_spmd

    nc = bacc.Bacc("TRN2", target_bir_lowering=False, num_devices=1)
    arrays, args = {}, []
    for name in _INS:
        a = np.ascontiguousarray(inputs[name])
        arrays[f"in_{name}"] = a
        args.append(nc.dram_tensor(f"in_{name}", a.shape, mybir.dt.from_np(a.dtype), kind="ExternalInput").ap())
    args.append(nc.dram_tensor("out_x", (1, TOK, D), F32, kind="ExternalOutput").ap())
    build(nc, *args)
    r = run_bass_kernel_spmd(nc, [arrays], core_ids=[0])
    return r.results[0]["out_x"]
```

```python
from contextlib import ExitStack

import concourse.bass as bass
import numpy as np
from concourse import mybir
from concourse.alu_op_type import AluOpType as ALU

F32 = mybir.dt.float32
F32R = mybir.dt.float32r
BF16 = mybir.dt.bfloat16
I32 = mybir.dt.int32
ACT = mybir.ActivationFunctionType
AX = mybir.AxisListType

P = 128
D = 1024
TOK = 256
CTX = 256
KC = D // P
HEADS, HD = 16, 64
GRID_W, ROWS, WIN = 64, 4, 16
RPB_ROWS, RPB_COLS = 15, 31
E, TOPK = 32, 4
SLOTS = 64
MAX_EXTRA = (TOK * TOPK) // SLOTS - 1
NCOL = E + MAX_EXTRA + 1
EPS = 1e-6
NEG = -1.0e30
LIMIT, ALPHA = 7.0, 1.702
HALF = 512

RING = 12
ADA0, QK, VV, ADA1, ADA2, WO, EXP = 0, 8, 16, 20, 28, 36, 40
PER = 12
BIAS_SLOTS = 8


def build(nc, x, c, ctx_in, c_ctx, ada_w, ada_b, norm_g, w_qkv, w_o, rpb, w_router, b_router,
          w_up, b_up, w_down, b_down, out):
    with ExitStack() as st:
        def sb(name, shape, dt=F32):
            return st.enter_context(nc.sbuf_tensor(name, shape, dt))

        def also(name, shape):
            with nc.sbuf_tensor(name, shape, F32R) as tensor:
                return tensor

        def sem(name):
            return st.enter_context(nc.semaphore(name))

        bank = [st.enter_context(nc.psum_tensor(f"bank{i}", [P, HALF], F32)) for i in range(8)]

        ring_low = also("ring_low", [P, RING, 2048])
        ring = sb("ring", [P, RING, 2048])
        tokens = sb("tokens", [P, 4, D])
        bias = tokens[:, :, :].rearrange("p a (b c) -> p (a b) c", c=512)
        hT_low_mem = also("hT_low", [P, KC * 512])
        hT_low = hT_low_mem[:, :].rearrange("p (k t) -> p k t", k=KC)
        hT_mem = sb("hT_mem", [P, KC * 512])
        hT = hT_mem[:, :].rearrange("p (k t) -> p k t", k=KC)
        oT = hT_mem[:, 0:2048].rearrange("p (k t) -> p k t", k=KC)
        acc = hT_mem[:, 2048:4096].rearrange("p (t d) -> p t d", t=2)
        kT_mem = sb("kT_mem", [P, KC * 512])
        kT = kT_mem[:, :].rearrange("p (k t) -> p k t", k=KC)
        x1 = kT_mem[:, 0:2048].rearrange("p (t d) -> p t d", t=2)
        h2T = kT_mem[:, 2048:4096].rearrange("p (k t) -> p k t", k=KC)
        q_mem = sb("q_mem", [P, KC * TOK])
        qT = q_mem[:, :].rearrange("p (k t) -> p k t", k=KC)
        h2 = q_mem[:, :].rearrange("p (t d) -> p t d", t=2)
        v_mem = sb("v_mem", [P, 4 * D])
        v = v_mem[:, :].rearrange("p (t d) -> p t d", t=4)
        xT = v_mem[:, 0:512].rearrange("p (j s) -> p j s", j=4)
        glu = v_mem[:, 512:1024]
        lin = v_mem[:, 1024:1536]
        sig = v_mem[:, 1536:2048]
        act = v_mem[:, 2048:2560]
        aT = v_mem[:, 2560:3072].rearrange("p (j s) -> p j s", j=4)
        y = v_mem[:, 3072:3584]
        combT = v_mem[:, 3584:3840].rearrange("p (t s) -> p t s", t=2)
        tmp = v_mem[:, 0:2048].rearrange("p (t d) -> p t d", t=2)
        junk = v_mem[:, 2048:3072]
        mod_high, mod = [], []
        for i in range(4):
            mod_high.append(also(f"mod_high{i}", [P, D]))
            mod.append(sb(f"mod{i}", [P, D]))
        gate1, shift2, scale2, gate2 = mod
        h_high = [m[:, :].rearrange("p (k t) -> p k t", k=2) for m in mod_high]
        probs_mem = mod[2], mod[3]
        probs = [m[:, 512 * i:512 * i + 512] for m in probs_mem for i in range(2)]
        gain_high = also("gain_high", [P, D])
        gain = sb("gain", [P, D])
        adab = sb("adab", [P, 3, HALF])
        rows = sb("rows", [P, HALF])
        pT_high = also("pT_high", [P, 1024])
        pT_mem = sb("pT_mem", [P, 1024])
        probsT = hT_mem[:, 2048:4096].rearrange("p (u k t) -> p u k t", u=4, k=4)
        wtmp = pT_mem[:, 0:2 * GRID_W].rearrange("p (i c) -> p i c", i=2)
        grow = pT_mem[0:KC, 640:768]
        crow, csig = pT_mem[0:2 * KC, 768:896], pT_mem[0:2 * KC, 896:1024]
        small = pT_mem[:, 0:12 * E].rearrange("p (i e) -> p i e", e=E)
        pick = pT_mem[:, 384:512].rearrange("p (t s) -> p t s", t=2)
        gT = pT_mem[0:E, 768:768 + TOK]
        comb = pT_mem[:, 512:768].rearrange("p (t a s) -> p t a s", t=2, a=2)
        w_high = [pT_high[:, :], gain_high[:, :]]
        ident = sb("ident", [P, P])
        ones = sb("ones", [P, P])
        before = sb("before", [P, P])
        sel = sb("sel", [P, 2, P])
        pmod = sb("pmod", [P, 1])
        slot_no = sb("slot_no", [P, 2, SLOTS])
        qcol = sb("qcol", [P, 1])
        wmask = sb("wmask", [P, GRID_W])
        neghalf = sb("neghalf", [P, 1])
        condT = sb("condT", [P, KC, 32])
        gcol = sb("gcol", [P, KC])
        scol, hcol = sb("scol", [P, 4, 2, 2]), sb("hcol", [P, 4, 2, 2])
        ssq = sb("ssq", [P, 4])
        ssq2 = sb("ssq2", [P, 2, 2])
        ssq3 = sb("ssq3", [P, 2])
        ssq4 = sb("ssq4", [P, 2])
        ms = sb("ms", [P, 8, 2])
        rstd = sb("rstd", [P, 8, 2])
        nmax = sb("nmax", [P, 4])
        psum_p = sb("psum_p", [P, 4])
        rinv = sb("rinv", [P, 4])
        wr = sb("wr", [P, KC, E])
        br = sb("br", [P, E])
        bup = tokens[0:E, 0:2, :].rearrange("p a d -> p (a d)")
        xe = hT_mem[:, 0:HALF]
        bup_parts = tokens[:, 2, :].bitcast(BF16)[0:3 * E, :]
        bup_part = hT_mem[0:E, 2048:3072].bitcast(BF16)
        bdown = tokens[0:E, 3, :]
        rank_e, gate_e2 = small[:, 0:2, :], small[:, 4:6, :]
        rT, blocks, first = mod[1][0:E, 0:TOK], mod[1][0:E, 256:260], mod[1][0:E, 260:261]
        owner, base, place, inside = (mod[1][0:E, a:a + NCOL] for a in (320, 384, 448, 512))
        owner3 = mod[1][0:3 * E, 576:576 + NCOL]
        bsel = mod[1][0:3 * E, 640:640 + SLOTS // 2].bitcast(BF16)
        rank_col = sb("rank_col", [P, 2, NCOL])
        gate_col = sb("gate_col", [P, 2, NCOL])
        block_no = sb("block_no", [E, NCOL])
        whose_i = sb("whose_i", [1, NCOL], I32)
        ends_i = sb("ends_i", [1, E], I32)

        slot_in = [sem(f"slot_in{i}") for i in range(RING)]
        ring_free = sem("ring_free")
        split_step, x_split, ctx_high, ctx_split = sem("split_step"), sem("x_split"), sem("ctx_high"), sem("ctx_split")
        w_split, split_used = sem("w_split"), sem("split_used")
        in_g0, gcol_ready, cols_ready = sem("in_g0"), sem("gcol_ready"), sem("cols_ready")
        rowsT_done, mod_dve, mod_act = sem("rowsT_done"), sem("mod_dve"), sem("mod_act")
        in_c, in_adab, in_x, in_ctx = sem("in_c"), sem("in_adab"), sem("in_x"), sem("in_ctx")
        in_router, in_gain, in_res = sem("in_router"), sem("in_gain"), sem("in_res")
        in_bdown, in_bup, out_done = sem("in_bdown"), sem("in_bup"), sem("out_done")
        in_bias = [sem(f"in_bias{i}") for i in range(BIAS_SLOTS)]
        pool_step = sem("pool_step")
        consts = sem("consts")
        dve_step = sem("dve_step")
        adab_zero = sem("adab_zero")
        c_sig, c_silu, c_T, cond_ready = sem("c_sig"), sem("c_silu"), sem("c_T"), sem("cond_ready")
        rows_ready, bc_done = sem("rows_ready"), sem("bc_done")
        bc_dve, bc_act = sem("bc_dve"), sem("bc_act")
        ssq_ready, ms_ready, rstd_ready = sem("ssq_ready"), sem("ms_ready"), sem("rstd_ready")
        mod_ready, tr_done, tr_act = sem("mod_ready"), sem("tr_done"), sem("tr_act")
        proj_done, proj_act, proj_dve = sem("proj_done"), sem("proj_act"), sem("proj_dve")
        bias_ready, bias_used = sem("bias_ready"), sem("bias_used")
        s_done, max_ready, exp_ready = sem("s_done"), sem("max_ready"), sem("exp_ready")
        sum_inv, prob_ready, pT_done, pT_ready = sem("sum_inv"), sem("prob_ready"), sem("pT_done"), sem("pT_ready")
        o_done, o_ready = sem("o_done"), sem("o_ready")
        wo_done, x1_ready, h2_ready = sem("wo_done"), sem("x1_ready"), sem("h2_ready")
        h2T_done, h2T_ready, logit_done = sem("h2T_done"), sem("h2T_ready"), sem("logit_done")
        mx_used = sem("mx_used")
        exp_gate_in, exp_gate = sem("exp_gate_in"), sem("exp_gate")
        mask_ready, gates_ready, rank_done = sem("mask_ready"), sem("gates_ready"), sem("rank_done")
        gT_done, gT_ready = sem("gT_done"), sem("gT_ready")
        counts_done, blocks_ready, first_done = sem("counts_done"), sem("blocks_ready"), sem("first_done")
        owner_ready, rT_done, rT_ready, tables_done = sem("owner_ready"), sem("rT_done"), sem("rT_ready"), sem("tables_done")
        tables_ready, rank_ready, bsel_ready, bup_split = sem("tables_ready"), sem("rank_ready"), sem("bsel_ready"), sem("bup_split")
        xe_ready, xeT_done = sem("xe_ready"), sem("xeT_done")
        pick_ready, comb_ready = sem("pick_ready"), sem("comb_ready")
        gather_done, xT_ready, combT_done, combT_ready = sem("gather_done"), sem("xT_ready"), sem("combT_done"), sem("combT_ready")
        up_done, glu_ready, lin_ready = sem("up_done"), sem("glu_ready"), sem("lin_ready")
        sig_ready, pre_ready, act_ready = sem("sig_ready"), sem("pre_ready"), sem("act_ready")
        aT_low, aT_high, aT_dve, aT_act = sem("aT_low"), sem("aT_high"), sem("aT_dve"), sem("aT_act")
        y_ready = sem("y_ready")
        part_done, acc_done = sem("part_done"), sem("acc_done")
        gated, fin_ready = sem("gated"), sem("fin_ready")

        def uses_before(slot):
            return len([n for n in range(EXP) if n % RING == slot])

        def chunk_here(eng, n):
            eng.wait_ge(slot_in[n % RING], 16 * (n // RING + 1))

        def expert_chunk_here(eng, e, j):
            s = (EXP + j) % RING
            eng.wait_ge(slot_in[s], e * 16 + 16 * (uses_before(s) + 1))

        def proj_here(eng, i):
            if i % 8 == 7:
                eng.wait_ge(split_used, i + 1)
            else:
                eng.wait_ge(proj_done, i + 1 - i // 8)

        def step_columns(s):
            what, k = s // KC, s % KC
            if what < 2:
                return (QK + k) % RING, slice(D * what, D * what + D)
            return (VV + k // 2) % RING, slice(D * (k % 2), D * (k % 2) + D)

        def by_row(t):
            return t.rearrange("p (r c) -> p r c", c=GRID_W)

        def backwards(t):
            return by_row(t)[:, :, ::-1]

        def wchunk(n):
            return ring[:, n % RING, :]

        def wpair(n, i):
            return ring[:, (n + i // 2) % RING, D * (i % 2):D * (i % 2) + D]

        def load_bias(eng, h):
            s = h % BIAS_SLOTS
            for r in range(ROWS):
                first = (h * RPB_ROWS + 7 - r) * RPB_COLS + 15 - (GRID_W - 1)
                src = bass.AP(rpb.tensor, first, [[1, GRID_W], [RPB_COLS, ROWS], [1, GRID_W]])
                half = 64 * (r % 2)
                dst = bias[half:half + 64, s, 256 * (r // 2):256 * (r // 2) + 256]
                eng.dma_start(dst.rearrange("p (i c) -> p i c", i=ROWS), src).then_inc(in_bias[s], 16)

        def number_of_blocks(eng):
            eng.wait_ge(tables_ready, 1)
            return eng.value_load(ends_i[0:1, E - 1:E], min_val=E, max_val=E + MAX_EXTRA)

        LAST_BANKS = ((6, 7), (0, 1))
        TR_BANK = [2 + i % 6 for i in range(8)]
        BC1 = [(0, 0), (0, 1), (0, 2), (0, 3)]
        UNITS = [(2 * p + j, t) for p in range(HEADS // 2) for t in range(2) for j in range(2)]
        MASK_AT = [9 + 2 * i for i in range(HEADS - BIAS_SLOTS)]
        ADA2_AT = 8

        block = st.enter_context(nc.Block())

        @block.sync
        def _(sp):
            ada_k = ada_w[0].rearrange("(k p) n -> k p n", p=P)
            qkv_k = w_qkv[0].rearrange("(k p) n -> k p n", p=P)
            v_2k = w_qkv[0].rearrange("(j k p) n -> j p k n", p=P, k=2)
            wo_2k = w_o[0].rearrange("(j k p) n -> j p k n", p=P, k=2)

            def source(n):
                if n < QK:
                    return ada_k[n - ADA0, :, 0:2048]
                if n < VV:
                    return qkv_k[n - QK, :, 0:2048]
                if n < ADA1:
                    return v_2k[n - VV, :, :, 2048:3072]
                if n < ADA2:
                    return ada_k[n - ADA1, :, 2048:4096]
                if n < WO:
                    return ada_k[n - ADA2, :, 4096:6144]
                return wo_2k[n - WO, :, :, :]

            def load(n):
                if n >= RING:
                    sp.wait_ge(ring_free, n - RING + 1)
                src = source(n)
                dst = wchunk(n)
                if len(src.shape) == 3:
                    dst = dst.rearrange("p (k n) -> p k n", k=2)
                sp.dma_start(dst, src).then_inc(slot_in[n % RING], 16)

            for n in range(ADA1):
                load(n)
            sp.wait_ge(tr_done, 8)
            for h in range(BIAS_SLOTS):
                load_bias(sp, h)
            for n in range(ADA1, EXP):
                load(n)
            for h in range(BIAS_SLOTS, HEADS):
                sp.wait_ge(bias_used, 4 * ((h - BIAS_SLOTS) // 2 + 1))
                load_bias(sp, h)

            up_k = w_up[0].rearrange("e (k p) n -> e k p n", p=P)
            down_2k = w_down[0].rearrange("e (j k p) n -> e j p k n", p=P, k=2)

            def expert(e, blocks_before):
                for j in range(PER):
                    sp.wait_ge(ring_free, blocks_before * PER + (EXP + j - RING + 1))
                    s = (EXP + j) % RING
                    if j < KC:
                        src = up_k[bass.ds(e, 1), j].rearrange("a p n -> (a p) n")
                        sp.dma_start(ring[:, s, :], src).then_inc(slot_in[s], 16)
                    else:
                        src = down_2k[bass.ds(e, 1), j - KC].rearrange("a p k n -> (a p) k n")
                        dst = ring[:, s, :].rearrange("p (k n) -> p k n", k=2)
                        sp.dma_start(dst, src).then_inc(slot_in[s], 16)

            expert(0, 0)
            sp.wait_ge(tables_ready, 1)
            with sp.Fori(1, E) as e:
                blocks_before = sp.value_load(ends_i[0:1, bass.ds(e - 1, 1)], min_val=1, max_val=E + MAX_EXTRA)
                expert(e, blocks_before)
            for t in range(2):
                sp.wait_ge(fin_ready, t + 1)
                sp.dma_start(out[0][P * t:P * t + P, :], tmp[:, t, :]).then_inc(out_done, 16)
            sp.wait_ge(out_done, 32)

        @block.gpsimd
        def _(pool):
            g = nc.gpsimd
            n = 0
            g.memset(ones[:, :], 1.0).then_inc(pool_step, 1)
            g.memset(ident[:, :], 0.0).then_inc(pool_step, 1)
            g.memset(neghalf[:, :], -0.5).then_inc(consts, 1)
            g.iota(slot_no[:, :, :], [[0, 2], [1, SLOTS]], base=0, channel_multiplier=0,
                   allow_small_or_imprecise_dtypes=True).then_inc(consts, 1)
            pool.wait_ge(pool_step, 2)
            for j in range(4):
                pool.wait_ge(consts, 2 + j)
                g.iota(pmod[32 * j:32 * j + 32, :], [[0, 1]], base=0, channel_multiplier=1,
                       allow_small_or_imprecise_dtypes=True).then_inc(consts, 1)
            pool.wait_ge(consts, 6)
            g.iota(block_no[:, :], [[1, NCOL]], base=0, channel_multiplier=0,
                   allow_small_or_imprecise_dtypes=True).then_inc(consts, 1)
            pool.wait_ge(consts, 7)
            g.affine_select(out=ident[:, :], in_=ident[:, :], compare_op=ALU.not_equal, fill=1.0, base=0,
                            pattern=[[-1, P]], channel_multiplier=1).then_inc(consts, 1)
            g.affine_select(out=before[:, :], in_=ones[:, :], compare_op=ALU.is_gt, fill=0.0, base=0,
                            pattern=[[1, P]], channel_multiplier=-1).then_inc(consts, 1)

            def powers(k, cols):
                pool.wait_ge(ms_ready, k + 1)
                g.tensor_tensor(rstd[:, k, 0:cols], ms[:, k, 0:cols], neghalf[:, 0:1].to_broadcast([P, cols]),
                                ALU.pow).then_inc(rstd_ready, 1)

            powers(0, 2)
            powers(1, 2)

            pool.wait_ge(consts, 9)
            pool.wait_ge(rstd_ready, 2)
            for j in range(2):
                pool.wait_ge(pool_step, 2 + j)
                g.iota(qcol[64 * j:64 * j + 64, :], [[0, 1]], base=GRID_W - 1, channel_multiplier=-1,
                       allow_small_or_imprecise_dtypes=True).then_inc(pool_step, 1)
            pool.wait_ge(pool_step, 4)
            g.iota(wmask[:, :], [[1, GRID_W]], base=0, channel_multiplier=0,
                   allow_small_or_imprecise_dtypes=True).then_inc(pool_step, 1)
            pool.wait_ge(pool_step, 5)
            g.tensor_scalar(qcol[:, :], qcol[:, :], -float(WIN // 2), 0.0, ALU.add, ALU.max).then_inc(pool_step, 1)
            pool.wait_ge(pool_step, 6)
            g.tensor_scalar(qcol[:, :], qcol[:, :], float(GRID_W - WIN), 0.0, ALU.min, ALU.add).then_inc(pool_step, 1)
            pool.wait_ge(pool_step, 7)
            g.tensor_scalar(wmask[:, :], wmask[:, :], qcol[:, 0:1], None, ALU.subtract).then_inc(pool_step, 1)
            pool.wait_ge(pool_step, 8)
            g.tensor_scalar(wtmp[:, 0, :], wmask[:, :], 0.0, NEG, ALU.is_lt, ALU.mult).then_inc(pool_step, 1)
            g.tensor_scalar(wtmp[:, 1, :], wmask[:, :], float(WIN - 1), NEG, ALU.is_gt, ALU.mult).then_inc(pool_step, 1)
            pool.wait_ge(pool_step, 10)
            g.tensor_tensor(wmask[:, :], wtmp[:, 0, :], wtmp[:, 1, :], ALU.add).then_inc(pool_step, 1)
            pool.wait_ge(pool_step, 11)

            for j in range(4):
                pool.wait_ge(ctx_high, j + 1)
                g.tensor_tensor(hT_low[:, 2 * j:2 * j + 2, TOK:2 * TOK], hT[:, 2 * j:2 * j + 2, TOK:2 * TOK],
                                h_high[j][:, :, TOK:2 * TOK], ALU.subtract).then_inc(ctx_split, 1)

            def gain_row(i):
                if i == 1:
                    pool.wait_ge(split_used, 24)
                else:
                    pool.wait_ge(bc_dve, 2 * i - 2)
                pool.dma_start(gain[:, :], norm_g[0][i:i + 1, :].to_broadcast([P, D])).then_inc(in_gain, 16)

            def mask_bias(h):
                s = h % BIAS_SLOTS
                pool.wait_ge(in_bias[s], 64 * (h // BIAS_SLOTS + 1))
                rows8 = bias[:, s, :].rearrange("p (i c) -> p i c", c=GRID_W)
                g.tensor_tensor(rows8, rows8, wmask[:, :].unsqueeze(1).to_broadcast([P, 8, GRID_W]),
                                ALU.add).then_inc(bias_ready, 1)

            for h in range(BIAS_SLOTS):
                mask_bias(h)
            gain_row(1)
            gain_row(2)
            for u in range(len(UNITS)):
                pool.wait_ge(sum_inv, u + 1)
                g.tensor_scalar(probs[u % 4], probs[u % 4], rinv[:, u % 4:u % 4 + 1], 1.0, ALU.mult,
                                ALU.mult).then_inc(prob_ready, 1)
                if u in MASK_AT:
                    mask_bias(BIAS_SLOTS + MASK_AT.index(u))
            gain_row(3)
            for k in range(2, 6):
                powers(k, 1)
            powers(6, 1)
            powers(7, 1)

        @block.scalar
        def _(sc):
            s = nc.scalar
            sc.dma_start(crow[0:KC, :], c.rearrange("a (k p) -> (a k) p", p=P)).then_inc(in_c, 16)
            sc.dma_start(crow[KC:2 * KC, :], c_ctx.rearrange("(k p) -> k p", p=P)).then_inc(in_c, 16)
            sc.dma_start(grow, norm_g[0][0:1, :].rearrange("a (k p) -> (a k) p", p=P)).then_inc(in_g0, 16)
            x_t = x[0].rearrange("(t p) d -> p t d", p=P)
            sc.dma_start(tokens[:, 0:2, :], x_t).then_inc(in_x, 16)
            sc.dma_start(tokens[:, 2:4, :], ctx_in[0].rearrange("(t p) d -> p t d", p=P)).then_inc(in_ctx, 16)
            sc.wait_ge(adab_zero, 1)
            for r in range(2):
                sc.dma_start(adab[r:r + 97:32, :, :], ada_b[0].rearrange("(g j n) -> j g n", g=3, j=4)).then_inc(in_adab, 16)
            sc.dma_start(wr[:, :, :], w_router[0].rearrange("(k p) e -> p k e", p=P)).then_inc(in_router, 16)
            sc.dma_start(br[:, :], b_router[0:1, :].to_broadcast([P, E])).then_inc(in_router, 16)

            sc.wait_ge(in_c, 32)
            s.activation(csig, crow, ACT.Sigmoid).then_inc(c_sig, 1)
            sc.wait_ge(c_T, 1)
            sc.wait_ge(cond_ready, 1)
            s.activation(gcol[:, :], bank[1][:, 2 * KC:3 * KC], ACT.Copy).then_inc(gcol_ready, 1)
            s.activation(condT[:, :, 0:2], bank[1][:, 0:2 * KC].rearrange("p (r k) -> p k r", r=2),
                         ACT.Copy).then_inc(cond_ready, 1)
            for t in range(4):
                sc.wait_ge(in_x if t < 2 else in_ctx, 16)
                s.activation(kT_mem[:, D * t:D * t + D], tokens[:, t, :], ACT.Square,
                             accum_out=ssq[:, t:t + 1]).then_inc(ssq_ready, 1)
            for i in range(8):
                sc.wait_ge(tr_done, i + 1)
                t, k0 = i // 2, 4 * (i % 2)
                s.activation(hT[:, k0:k0 + 4, P * t:P * t + P], bank[TR_BANK[i]][:, :].rearrange("p (k t) -> p k t", k=4),
                             ACT.Copy).then_inc(tr_act, 1)
            sc.wait_ge(cols_ready, 4)
            sc.wait_ge(tr_act, 8)
            for part in range(2):
                for k in range(1, KC, 2):
                    h = hT[:, k, TOK * part:TOK * part + TOK]
                    s.activation(h, h, ACT.Identity, bias=hcol[:, k % 4, k // 4, part:part + 1],
                                 scale=scol[:, k % 4, k // 4, part:part + 1]).then_inc(mod_act, 1)
            for i in range(0, 24, 2):
                proj_here(sc, i)
                if i < 8:
                    s.activation(by_row(qT[:, i, :]), backwards(bank[i % 8][:, 0:TOK]), ACT.Copy, scale=HD ** -0.5).then_inc(proj_act, 1)
                elif i < 16:
                    s.activation(kT[:, i - 8, :], bank[i % 8][:, :], ACT.Copy).then_inc(proj_act, 1)
                else:
                    s.activation(v[:, (i - 16) // 2, 0:HALF], bank[i % 8][:, :], ACT.Copy).then_inc(proj_act, 1)

            def take_shift2():
                for i in range(2):
                    sc.wait_ge(bc_done, 2 + i + 1)
                    s.activation(shift2[:, HALF * i:HALF * i + HALF], bank[5 + i][:, :], ACT.Copy).then_inc(bc_act, 1)

            def softmax_exp(u):
                sc.wait_ge(max_ready, u + 1)
                if u >= 4:
                    sc.wait_ge(pT_done, u - 3)
                s.activation(probs[u % 4], bank[u % 3][:, :], ACT.Exp, bias=nmax[:, u % 4:u % 4 + 1],
                             accum_out=psum_p[:, u % 4:u % 4 + 1]).then_inc(exp_ready, 1)

            def take_probsT(u):
                sc.wait_ge(pT_done, u + 1)
                if u >= 4:
                    sc.wait_ge(o_done, u // 2 - 1)
                s.activation(probsT[:, u % 4, :, :], bank[3 + u % 2][:, :].rearrange("p (k t) -> p k t", k=4),
                             ACT.Copy).then_inc(pT_ready, 1)

            for u in range(len(UNITS)):
                softmax_exp(u)
                if u == 1:
                    take_shift2()
                if u >= 2:
                    take_probsT(u - 2)
            take_probsT(len(UNITS) - 2)
            take_probsT(len(UNITS) - 1)
            def take_exp_gate(t):
                sc.wait_ge(exp_gate_in, t + 1)
                s.activation(small[:, 8 + t, :], small[:, t, :], ACT.Exp, bias=nmax[:, t:t + 1]).then_inc(exp_gate, 1)

            sc.wait_ge(s_done, len(UNITS))
            sc.dma_start(x1, x_t).then_inc(in_res, 16)
            sc.wait_ge(bias_used, len(UNITS))
            sc.dma_start(bup, b_up[0]).then_inc(in_bup, 16)
            sc.dma_start(bdown, b_down[0]).then_inc(in_bdown, 16)
            for t in range(2):
                if t == 1:
                    sc.wait_ge(ssq_ready, 7)
                for i in range(2):
                    if (t, i) != (1, 1):
                        sc.wait_ge(wo_done, 2 * t + i + 1)
                    else:
                        sc.wait_ge(ring_free, EXP)
                    s.activation(junk[:, HALF * i:HALF * i + HALF], bank[4 + 2 * t + i][:, :], ACT.Square,
                                 accum_out=ssq2[:, t, i:i + 1]).then_inc(ssq_ready, 1)
                sc.wait_ge(x1_ready, t + 1)
                sc.wait_ge(ssq_ready, 6 + 3 * t)
                s.activation(junk, x1[:, t, :], ACT.Square, accum_out=ssq3[:, t:t + 1]).then_inc(ssq_ready, 1)
            for t in range(2):
                for i in range(2 * t, 2 * t + 2):
                    sc.wait_ge(h2T_done, i + 1)
                    k0 = 4 * (i % 2)
                    s.activation(h2T[:, k0:k0 + 4, P * t:P * t + P], bank[i][:, :].rearrange("p (k t) -> p k t", k=4),
                                 ACT.Copy).then_inc(h2T_ready, 1)
                if t == 1:
                    take_exp_gate(0)
            take_exp_gate(1)

            def take_xe(b):
                sc.wait_ge(gather_done, b + 1)
                s.activation(xe, bank[3][:, :], ACT.Copy).then_inc(xe_ready, 1)

            def take_xT(b):
                sc.wait_ge(xeT_done, b + 1)
                s.activation(xT, bank[3][:, :].rearrange("p (j s) -> p j s", j=4), ACT.Copy).then_inc(xT_ready, 1)

            take_xe(0)
            sc.wait_ge(gT_done, 1)
            s.activation(gT, bank[7][0:E, 0:TOK], ACT.Copy).then_inc(gT_ready, 1)
            take_xT(0)
            sc.wait_ge(rT_done, 1)
            s.activation(rT, bank[7][0:E, 0:TOK], ACT.Copy).then_inc(rT_ready, 1)

            def block_step(b, is_first=False):
                sc.wait_ge(glu_ready, b + 1)
                s.activation(sig, glu, ACT.Sigmoid, scale=ALPHA).then_inc(sig_ready, 1)
                take_xe(b + 1)
                sc.wait_ge(combT_done, b + 1)
                if not is_first:
                    sc.wait_ge(part_done, b * 4 + 4)
                s.activation(combT, bank[4][:, 0:TOK].rearrange("p (t s) -> p t s", t=2), ACT.Copy).then_inc(combT_ready, 1)
                sc.wait_ge(aT_high, b + 1)
                s.activation(aT[:, 2:4, :], bank[4][:, 0:TOK].rearrange("p (j s) -> p j s", j=2),
                             ACT.Copy).then_inc(aT_act, 1)
                take_xT(b + 1)
                sc.wait_ge(ring_free, b * PER + (EXP + PER))
                s.activation(y, bank[2][:, :], ACT.Copy).then_inc(y_ready, 1)

            block_step(0, is_first=True)
            last_block = number_of_blocks(sc)
            with sc.Fori(1, last_block) as b:
                block_step(b)
            for t in range(2):
                sc.wait_ge(acc_done, last_block * 4 + (2 * t + 2))
                sc.wait_ge(ssq_ready, 10 + t)
                s.activation(junk, acc[:, t, :], ACT.Square,
                             accum_out=ssq4[:, t:t + 1]).then_inc(ssq_ready, 1)

        @block.vector
        def _(ve):
            d = nc.vector
            steps = [0]

            def step(ins):
                ins.then_inc(dve_step, 1)
                steps[0] += 1
                ve.wait_ge(dve_step, steps[0])

            d.memset(adab[:, :, :], 0.0).then_inc(adab_zero, 1)
            d.memset(condT[:, :, :], 0.0).then_inc(cond_ready, 1)
            ve.wait_ge(c_sig, 1)
            d.tensor_tensor(csig, csig, crow, ALU.mult).then_inc(c_silu, 1)
            ve.wait_ge(pool_step, 2)
            ve.wait_ge(consts, 9)
            d.tensor_scalar(sel[:, 0, :], ones[:, :], 1.0, pmod[:, 0:1], ALU.subtract, ALU.is_equal)
            step(d.tensor_scalar(sel[:, 1, :], ones[:, :], pmod[:, 0:1], None, ALU.is_equal))

            def mean_squares(k, src, cols):
                d.tensor_scalar(ms[:, k, 0:cols], src, 1.0 / D, EPS, ALU.mult, ALU.add).then_inc(ms_ready, 1)

            for part in range(2):
                ve.wait_ge(ssq_ready, 2 * part + 2)
                mean_squares(part, ssq[:, 2 * part:2 * part + 2], 2)
                ve.wait_ge(rstd_ready, part + 1)
                for t in range(2 * part, 2 * part + 2):
                    d.tensor_scalar(tokens[:, t, :], tokens[:, t, :], rstd[:, part, t % 2:t % 2 + 1], None,
                                    ALU.mult).then_inc(mod_ready, 1)

            def take_rows(g):
                ve.wait_ge(ring_free, (ADA0, ADA1, ADA2)[g] + KC)
                if g == 0:
                    ve.wait_ge(in_adab, 32)
                else:
                    ve.wait_ge(rowsT_done if g == 1 else bc_done, (1, 4)[g - 1])
                b = (0, 7, 7)[g]
                d.tensor_tensor(rows[:, :], bank[b][:, :], adab[:, g, :], ALU.add).then_inc(rows_ready, 1)

            take_rows(0)
            ve.wait_ge(gcol_ready, 1)
            ve.wait_ge(rowsT_done, 1)
            cols = bank[1][:, :].rearrange("p (m j s) -> p m j s", m=4, j=4)
            gains = gcol[:, :].rearrange("p (j m) -> p m j", m=4)
            for part in range(2):
                d.scalar_tensor_tensor(scol[:, :, :, part], cols[:, :, 2:4, part], 1.0, gains, ALU.add, ALU.mult).then_inc(cols_ready, 1)
                d.tensor_copy(hcol[:, :, :, part], cols[:, :, 0:2, part]).then_inc(cols_ready, 1)
            ve.wait_ge(cols_ready, 4)
            ve.wait_ge(tr_act, 8)

            def modulate_even(part):
                for k in range(0, KC, 2):
                    h = hT[:, k, TOK * part:TOK * part + TOK]
                    d.tensor_scalar(h, h, scol[:, k % 4, k // 4, part:part + 1], hcol[:, k % 4, k // 4, part:part + 1],
                                    ALU.mult, ALU.add).then_inc(mod_dve, 1)

            def split_x(j):
                ve.wait_ge(mod_dve, j + 1)
                ve.wait_ge(mod_act, j + 1)
                h = hT[:, 2 * j:2 * j + 2, 0:TOK]
                step(d.tensor_copy(h_high[j][:, :, 0:TOK], h))
                d.tensor_tensor(hT_low[:, 2 * j:2 * j + 2, 0:TOK], h, h_high[j][:, :, 0:TOK], ALU.subtract).then_inc(x_split, 1)

            def high_ctx(j):
                ve.wait_ge(mod_dve, 4 + j + 1)
                ve.wait_ge(mod_act, 4 + j + 1)
                d.tensor_copy(h_high[j][:, :, TOK:2 * TOK], hT[:, 2 * j:2 * j + 2, TOK:2 * TOK]).then_inc(ctx_high, 1)

            def split_weights(s):
                if s < 8:
                    chunk_here(ve, QK + s)
                elif s >= 16 and s % 2 == 0:
                    chunk_here(ve, VV + (s - 16) // 2)
                if s >= 2:
                    ve.wait_ge(split_used, s - 1)
                slot, cols = step_columns(s)
                w = ring[:, slot, cols]
                step(d.tensor_copy(w_high[s % 2], w))
                d.tensor_tensor(ring_low[:, slot, cols], w, w_high[s % 2], ALU.subtract).then_inc(w_split, 1)

            def take_projections(what):
                for i in range(8 * what + 1, 8 * what + 8, 2):
                    proj_here(ve, i)
                    if what == 0:
                        d.tensor_scalar(by_row(qT[:, i, :]), backwards(bank[i % 8][:, 0:TOK]), HD ** -0.5, None, ALU.mult).then_inc(proj_dve, 1)
                    elif what == 1:
                        d.tensor_copy(kT[:, i - 8, :], bank[i % 8][:, :]).then_inc(proj_dve, 1)
                    else:
                        d.tensor_copy(v[:, (i - 16) // 2, HALF:D], bank[i % 8][:, :]).then_inc(proj_dve, 1)

            modulate_even(0)
            split_x(0)
            ve.wait_ge(pool_step, 11)
            split_weights(0)
            split_x(1)
            split_weights(1)
            split_x(2)
            split_x(3)
            split_weights(2)
            modulate_even(1)
            split_weights(3)
            for j in range(4):
                high_ctx(j)
                split_weights(4 + j)
            for what in range(1, 3):
                split_weights(8 * what)
                take_projections(what - 1)
                for k in range(1, KC):
                    split_weights(8 * what + k)
            take_projections(2)

            def make_gate1():
                ve.wait_ge(in_gain, 16)
                for i in range(2):
                    ve.wait_ge(bc_done, i + 1)
                    h = slice(HALF * i, HALF * i + HALF)
                    d.tensor_tensor(gate1[:, h], bank[3 + i][:, :], gain[:, h], ALU.mult).then_inc(bc_dve, 1)

            def scores(u):
                h, t = UNITS[u]
                ve.wait_ge(s_done, u + 1)
                if t == 0:
                    ve.wait_ge(bias_ready, h + 1)
                sl = bank[u % 3][:, 0:256]
                d.tensor_tensor(sl, sl, bias[:, h % BIAS_SLOTS, 256 * t:256 * t + 256], ALU.add).then_inc(bias_used, 1)
                ve.wait_ge(bias_used, u + 1)
                if u >= 4:
                    ve.wait_ge(exp_ready, u - 3)
                d.tensor_reduce(nmax[:, u % 4:u % 4 + 1], bank[u % 3][:, :], AX.X, ALU.max, negate=True).then_inc(max_ready, 1)

            def invert(u):
                ve.wait_ge(exp_ready, u + 1)
                if u >= 4:
                    ve.wait_ge(prob_ready, u - 3)
                d.reciprocal(rinv[:, u % 4:u % 4 + 1], psum_p[:, u % 4:u % 4 + 1]).then_inc(sum_inv, 1)

            def take_o(p):
                ve.wait_ge(o_done, 2 * p + 2)
                d.tensor_copy(by_row(oT[:, p, :]), backwards(bank[5 + p % 2][:, 0:TOK])).then_inc(o_ready, 1)

            for u in range(len(UNITS)):
                scores(u)
                if u >= 1:
                    invert(u - 1)
                if u >= 7 and u % 4 == 3:
                    take_o((u - 7) // 4)
                if u == 1:
                    take_rows(1)
                    make_gate1()
                if u == ADA2_AT + 1:
                    take_rows(2)
            invert(len(UNITS) - 1)
            take_o(HEADS // 2 - 1)
            ve.wait_ge(in_gain, 32)
            for i in range(2):
                ve.wait_ge(bc_done, 4 + i + 1)
                h = slice(HALF * i, HALF * i + HALF)
                d.scalar_tensor_tensor(scale2[:, h], bank[i][:, :], 1.0, gain[:, h], ALU.add, ALU.mult).then_inc(bc_dve, 1)
            ve.wait_ge(in_bup, 16)
            step(d.tensor_copy(bup_parts[0:E, :], bup))
            step(d.tensor_tensor(bup, bup, bup_parts[0:E, :], ALU.subtract))
            step(d.tensor_copy(bup_part, bup))
            step(d.tensor_tensor(bup, bup, bup_part, ALU.subtract))
            d.tensor_copy(bup_parts[E:2 * E, :], bup_part)
            d.tensor_copy(bup_parts[2 * E:3 * E, :], bup).then_inc(bup_split, 1)
            ve.wait_ge(in_gain, 48)
            for i in range(2):
                ve.wait_ge(bc_done, 6 + i + 1)
                h = slice(HALF * i, HALF * i + HALF)
                d.tensor_tensor(gate2[:, h], bank[2 + i][:, :], gain[:, h], ALU.mult).then_inc(bc_dve, 1)
            ve.wait_ge(in_res, 16)
            ve.wait_ge(bc_dve, 6)
            for t in range(2):
                for i in range(2):
                    ve.wait_ge(ssq_ready, 5 + 3 * t + i)
                    h = slice(HALF * i, HALF * i + HALF)
                    d.tensor_tensor(tmp[:, t, h], bank[4 + 2 * t + i][:, :], gate1[:, h], ALU.mult).then_inc(mx_used, 1)
                step(d.tensor_tensor(ssq2[:, t, 0:1], ssq2[:, t, 0:1], ssq2[:, t, 1:2], ALU.add))
                mean_squares(2 + 2 * t, ssq2[:, t, 0:1], 1)
                ve.wait_ge(mx_used, 2 * t + 2)
                ve.wait_ge(rstd_ready, 3 + 2 * t)
                d.scalar_tensor_tensor(x1[:, t, :], tmp[:, t, :], rstd[:, 2 + 2 * t, 0:1], x1[:, t, :],
                                       ALU.mult, ALU.add).then_inc(x1_ready, 1)
                ve.wait_ge(x1_ready, t + 1)
                step(d.tensor_tensor(h2[:, t, :], x1[:, t, :], scale2[:, :], ALU.mult))
                ve.wait_ge(ssq_ready, 7 + 3 * t)
                mean_squares(3 + 2 * t, ssq3[:, t:t + 1], 1)
                ve.wait_ge(rstd_ready, 4 + 2 * t)
                d.scalar_tensor_tensor(h2[:, t, :], h2[:, t, :], rstd[:, 3 + 2 * t, 0:1], shift2[:, :],
                                       ALU.mult, ALU.add).then_inc(h2_ready, 1)

            logit, top, over, tie, gate_e, mask = (small[:, 2 * i:2 * i + 2, :] for i in range(6))
            ve.wait_ge(in_router, 32)
            for t in range(2):
                ve.wait_ge(logit_done, t + 1)
                step(d.tensor_tensor(logit[:, t, :], bank[4 + t][:, 0:E], br[:, :], ALU.add))
                step(d.max(top[:, t, 0:8], logit[:, t, :]))
                d.tensor_scalar(nmax[:, t:t + 1], top[:, t, 0:1], -1.0, None, ALU.mult).then_inc(exp_gate_in, 1)
                d.tensor_scalar(over[:, t, :], logit[:, t, :], top[:, t, TOPK - 1:TOPK], None, ALU.is_gt)
                step(d.tensor_scalar(tie[:, t, :], logit[:, t, :], top[:, t, TOPK - 1:TOPK], None, ALU.is_equal))
                step(d.tensor_reduce(top[:, t, 8:9], over[:, t, :], AX.X, ALU.add, negate=True))
                d.tensor_scalar(top[:, t, 9:10], top[:, t, 8:9], float(TOPK), None, ALU.add)
                step(d.tensor_tensor_scan(mask[:, t, :], ones[:, 0:E], tie[:, t, :], 0.0, ALU.mult, ALU.add))
                step(d.tensor_scalar(mask[:, t, :], mask[:, t, :], top[:, t, 9:10], None, ALU.is_le))
                step(d.tensor_tensor(mask[:, t, :], mask[:, t, :], tie[:, t, :], ALU.mult))
                d.tensor_tensor(mask[:, t, :], mask[:, t, :], over[:, t, :], ALU.add).then_inc(mask_ready, 1)
                ve.wait_ge(mask_ready, t + 1)
                ve.wait_ge(exp_gate, t + 1)
                step(d.tensor_tensor(gate_e[:, t, :], gate_e[:, t, :], mask[:, t, :], ALU.mult))
                step(d.tensor_reduce(top[:, t, 10:11], gate_e[:, t, :], AX.X, ALU.add))
                step(d.reciprocal(top[:, t, 11:12], top[:, t, 10:11]))
                d.tensor_scalar(gate_e2[:, t, :], gate_e[:, t, :], top[:, t, 11:12], None, ALU.mult).then_inc(gates_ready, 1)
            ve.wait_ge(gates_ready, 2)
            ve.wait_ge(rank_done, 1)
            for t in range(2):
                step(d.scalar_tensor_tensor(rank_e[:, t, :], bank[6][:, E * t:E * t + E], 1.0, mask[:, t, :], ALU.add, ALU.mult))
                d.tensor_scalar(rank_e[:, t, :], rank_e[:, t, :], -1.0, None, ALU.add).then_inc(rank_ready, 1)
            ve.wait_ge(rank_ready, 2)

            def make_pick(ranks, b):
                for t in range(2):
                    ins = d.tensor_scalar(pick[:, t, :], slot_no[:, 0, :], ranks[:, t, bass.ds(b, 1)], None, ALU.is_equal)
                ins.then_inc(pick_ready, 1)

            def make_comb(ranks, gates, b):
                for t in range(2):
                    ins = d.tensor_scalar(comb[:, t, :, :], slot_no[:, :, :], ranks[:, t, bass.ds(b, 1)],
                                          gates[:, t, bass.ds(b, 1)], ALU.is_equal, ALU.mult)
                ins.then_inc(comb_ready, 1)

            def make_bsel(b):
                d.tensor_copy(bsel, owner3[:, bass.ds(b, 1)].to_broadcast([3 * E, SLOTS])).then_inc(bsel_ready, 1)

            make_pick(rank_e, 0)
            ve.wait_ge(counts_done, 1)
            step(d.tensor_copy(blocks[:, 3:4], bank[6][0:E, 0:1]))
            step(d.tensor_scalar(blocks[:, 0:1], blocks[:, 3:4], float(SLOTS), 1.0, ALU.is_gt, ALU.add))
            step(d.tensor_scalar(blocks[:, 1:2], blocks[:, 3:4], float(2 * SLOTS), blocks[:, 0:1], ALU.is_gt, ALU.add))
            d.tensor_scalar(blocks[:, 2:3], blocks[:, 3:4], float(3 * SLOTS), blocks[:, 1:2], ALU.is_gt, ALU.add).then_inc(blocks_ready, 1)
            make_comb(rank_e, gate_e2, 0)
            ve.wait_ge(first_done, 1)
            ve.wait_ge(blocks_ready, 1)
            step(d.tensor_copy(first, bank[6][0:E, 0:1]))
            step(d.tensor_scalar(place, block_no[:, :], first, None, ALU.subtract))
            step(d.tensor_scalar(inside, place, blocks[:, 2:3], None, ALU.is_lt))
            step(d.scalar_tensor_tensor(owner, place, 0.0, inside, ALU.is_ge, ALU.mult))
            d.scalar_tensor_tensor(base, place, -float(SLOTS), owner, ALU.mult, ALU.mult).then_inc(owner_ready, 1)
            for i in range(3):
                ins = d.tensor_copy(owner3[E * i:E * i + E, :], owner)
            step(ins)
            make_bsel(0)
            ve.wait_ge(tables_done, 1)
            d.tensor_copy(whose_i[:, :], bank[6][0:1, 64:64 + NCOL])
            d.tensor_copy(ends_i[:, :], bank[6][0:1, 128:128 + E])
            d.tensor_copy(rank_col[:, :, :], bank[5][:, 0:2 * NCOL].rearrange("p (t b) -> p t b", t=2))
            ins = d.tensor_copy(gate_col[:, :, :], bank[5][:, 2 * NCOL:4 * NCOL].rearrange("p (t b) -> p t b", t=2))
            ins.then_inc(tables_ready, 1)
            ve.wait_ge(tables_ready, 1)

            def add_part(t, b, is_first=False, banks=(6, 7)):
                ve.wait_ge(part_done, b * 4 + (2 * t + 2))
                for n in range(2):
                    dst = acc[:, t, HALF * n:HALF * n + HALF]
                    if is_first:
                        d.tensor_copy(dst, bank[banks[n]][:, :]).then_inc(acc_done, 1)
                    else:
                        d.tensor_tensor(dst, dst, bank[banks[n]][:, :], ALU.add).then_inc(acc_done, 1)

            def block_step(b, is_first=False):
                ve.wait_ge(gather_done, b + 1)
                make_pick(rank_col, b + 1)
                ve.wait_ge(up_done, b + 1)
                d.tensor_scalar(glu, bank[0][:, :], LIMIT, None, ALU.min).then_inc(glu_ready, 1)
                d.tensor_scalar(lin, bank[1][:, :], LIMIT, -LIMIT, ALU.min, ALU.max).then_inc(lin_ready, 1)
                ve.wait_ge(glu_ready, b + 1)
                ve.wait_ge(lin_ready, b + 1)
                d.scalar_tensor_tensor(act, lin, 1.0, glu, ALU.add, ALU.mult).then_inc(pre_ready, 1)
                if not is_first:
                    ve.wait_ge(acc_done, b * 4)
                add_part(0, b, is_first)
                ve.wait_ge(pre_ready, b + 1)
                ve.wait_ge(sig_ready, b + 1)
                d.tensor_tensor(act, act, sig, ALU.mult).then_inc(act_ready, 1)
                make_bsel(b + 1)
                ve.wait_ge(aT_low, b + 1)
                d.tensor_copy(aT[:, 0:2, :], bank[5][:, 0:TOK].rearrange("p (j s) -> p j s", j=2)).then_inc(aT_dve, 1)
                add_part(1, b, is_first)
                ve.wait_ge(combT_done, b + 1)
                make_comb(rank_col, gate_col, b + 1)

            block_step(0, is_first=True)
            last_block = number_of_blocks(ve)
            with ve.Fori(1, last_block) as b:
                block_step(b)
            ve.wait_ge(acc_done, last_block * 4)
            for t in range(2):
                add_part(t, last_block, banks=LAST_BANKS[t])
                ve.wait_ge(acc_done, last_block * 4 + (2 * t + 2))
                d.tensor_tensor(tmp[:, t, :], acc[:, t, :], gate2[:, :], ALU.mult).then_inc(gated, 1)
                ve.wait_ge(ssq_ready, 11 + t)
                mean_squares(6 + t, ssq4[:, t:t + 1], 1)
                ve.wait_ge(gated, t + 1)
                ve.wait_ge(rstd_ready, 7 + t)
                d.scalar_tensor_tensor(tmp[:, t, :], tmp[:, t, :], rstd[:, 6 + t, 0:1], x1[:, t, :],
                                       ALU.mult, ALU.add).then_inc(fin_ready, 1)

        @block.tensor
        def _(pe):
            mm, tr = nc.tensor.matmul, nc.tensor.transpose

            pe.wait_ge(consts, 9)
            pe.wait_ge(c_silu, 1)
            pe.wait_ge(in_g0, 16)
            tr(bank[1][:, 2 * KC:3 * KC], grow, ident[0:KC, 0:KC])
            tr(bank[1][:, 0:2 * KC], csig, ident[0:2 * KC, 0:2 * KC]).then_inc(c_T, 1)
            pe.wait_ge(cond_ready, 2)

            def transpose_tokens(i):
                t, k0 = i // 2, 4 * (i % 2)
                pe.wait_ge(mod_ready, t + 1)
                if i >= 6:
                    pe.wait_ge(tr_act, i - 5)
                for j in range(4):
                    last = tr(bank[TR_BANK[i]][:, P * j:P * j + P], tokens[:, t, P * (k0 + j):P * (k0 + j) + P], ident[:, :])
                last.then_inc(tr_done, 1)

            def ada(g, b):
                for k in range(KC):
                    n = (ADA0, ADA1, ADA2)[g] + k
                    chunk_here(pe, n)
                    for j in range(4):
                        last = mm(bank[b][32 * j:32 * j + 32, :], condT[:, k, :], wchunk(n)[:, HALF * j:HALF * j + HALF],
                                  start=k == 0, stop=k == KC - 1)
                    last.then_inc(ring_free, 1)
                    if g == 0:
                        for i in {3: (0, 1), 4: (2, 3), 6: (4, 5), 7: (6, 7)}.get(k, ()):
                            transpose_tokens(i)

            def broadcast(jobs, banks):
                for (r, j), b in zip(jobs, banks):
                    mm(bank[b][:, :], sel[32 * j:32 * j + 32, r, :], rows[32 * j:32 * j + 32, :],
                       start=True, stop=True).then_inc(bc_done, 1)

            ada(0, 0)
            pe.wait_ge(rows_ready, 1)
            for m in range(4):
                last = tr(bank[1][:, P * m:P * m + P], rows[:, P * m:P * m + P], ident[:, :])
            last.then_inc(rowsT_done, 1)
            for s in range(24):
                what, k = s // KC, s % KC
                pe.wait_ge(w_split, s + 1)
                if what == 0:
                    pe.wait_ge(x_split, k // 2 + 1)
                elif what == 1:
                    pe.wait_ge(ctx_split, k // 2 + 1)
                slot, cols = step_columns(s)
                w_parts = ring_low[:, slot, cols], w_high[s % 2], w_high[s % 2]
                h_parts = h_high[k // 2][:, k % 2, :], h_high[k // 2][:, k % 2, :], hT_low[:, k, :]
                for i in range(8):
                    n = 8 * what + i
                    if what > 0 and k == 0:
                        pe.wait_ge(proj_act if n % 2 == 0 else proj_dve, (n - 8) // 2 + 1)
                    for part, (w, h) in enumerate(zip(w_parts, h_parts)):
                        if what < 2:
                            cols = TOK * (what + 1)
                            out_, left, right = bank[i][:, 0:cols], w[:, P * i:P * i + P], h[:, 0:cols]
                        else:
                            t, j = i // 2, i % 2
                            out_, left, right = bank[i][:, :], h[:, P * t:P * t + P], w[:, HALF * j:HALF * j + HALF]
                        last = mm(out_, left, right,
                                  start=k == 0 and part == 0, stop=k == KC - 1 and part == 2)
                        if part == 0 and i == 7 and (what == 1 or (what == 2 and k % 2 == 1)):
                            last.then_inc(ring_free, 1)
                    if i == 7:
                        last.then_inc(split_used, 1)
                    elif k == KC - 1:
                        last.then_inc(proj_done, 1)

            def score(u):
                h, t = UNITS[u]
                p0 = HD * (h % 2)
                if u >= 3:
                    pe.wait_ge(exp_ready, u - 2)
                mm(bank[u % 3][:, :], qT[p0:p0 + HD, h // 2, P * t:P * t + P], kT[p0:p0 + HD, h // 2, :],
                   start=True, stop=True).then_inc(s_done, 1)

            def transpose_probs(u):
                pe.wait_ge(prob_ready, u + 1)
                if u >= 2:
                    pe.wait_ge(pT_ready, u - 1)
                for kc in range(4):
                    last = tr(bank[3 + u % 2][:, P * kc:P * kc + P], probs[u % 4][:, P * kc:P * kc + P], ident[:, :])
                last.then_inc(pT_done, 1)

            def mix(m):
                p, t = m // 2, m % 2
                pe.wait_ge(pT_ready, 2 * m + 2)
                if p >= 2:
                    pe.wait_ge(o_ready, p - 1)
                for kc in range(4):
                    for j in range(2):
                        h = 2 * p + j
                        last = mm(bank[5 + p % 2][HD * j:HD * j + HD, P * t:P * t + P], v[:, kc, HD * h:HD * h + HD],
                                  probsT[:, (2 * m + j) % 4, kc, :], start=kc == 0, stop=kc == 3)
                last.then_inc(o_done, 1)

            pe.wait_ge(proj_act, 12)
            pe.wait_ge(proj_dve, 12)
            score(0)
            score(1)
            ada(1, 7)
            for u in range(len(UNITS)):
                if u == ADA2_AT:
                    ada(2, 7)
                if u + 2 < len(UNITS):
                    score(u + 2)
                if u == 0:
                    pe.wait_ge(rows_ready, 2)
                    pe.wait_ge(dve_step, 1)
                    broadcast(BC1, range(3, 7))
                if u == 1:
                    pe.wait_ge(bc_dve, 2)
                    pe.wait_ge(bc_act, 2)
                if u >= 1:
                    transpose_probs(u - 1)
                if u >= 3 and u % 2 == 1:
                    mix((u - 3) // 2)
            transpose_probs(len(UNITS) - 1)
            mix(len(UNITS) // 2 - 1)

            pe.wait_ge(rows_ready, 3)
            broadcast(BC1, range(4))
            pe.wait_ge(o_ready, HEADS // 2)
            for t in range(2):
                for i in range(2):
                    for k in range(KC):
                        if t == 0 and i == 0 and k % 2 == 0:
                            chunk_here(pe, WO + k // 2)
                        last = mm(bank[4 + 2 * t + i][:, :], oT[:, k, P * t:P * t + P],
                                  wpair(WO, k)[:, HALF * i:HALF * i + HALF], start=k == 0, stop=k == KC - 1)
                        if t == 1 and i == 1 and k % 2 == 1:
                            last.then_inc(ring_free, 1)
                    if (t, i) != (1, 1):
                        last.then_inc(wo_done, 1)
            pe.wait_ge(bc_dve, 6)
            pe.wait_ge(in_router, 32)
            for t in range(2):
                pe.wait_ge(h2_ready, t + 1)
                for i in range(2 * t, 2 * t + 2):
                    for j in range(4):
                        k = 4 * (i % 2) + j
                        last = tr(bank[i][:, P * j:P * j + P], h2[:, t, P * k:P * k + P], ident[:, :])
                    last.then_inc(h2T_done, 1)
                pe.wait_ge(mx_used, 2 * t + 2)
                for k in range(KC):
                    if k % 4 == 0:
                        pe.wait_ge(h2T_ready, 2 * t + k // 4 + 1)
                    last = mm(bank[4 + t][:, 0:E], h2T[:, k, P * t:P * t + P], wr[:, k, :], start=k == 0, stop=k == KC - 1)
                last.then_inc(logit_done, 1)
            pe.wait_ge(mask_ready, 2)
            mask = small[:, 10:12, :]
            mm(bank[6][:, 0:E], before[:, :], mask[:, 0, :], start=True, stop=True)
            mm(bank[6][:, E:2 * E], before[:, :], mask[:, 1, :], start=True, stop=False)
            mm(bank[6][:, E:2 * E], ones[:, :], mask[:, 0, :], start=False, stop=True)
            mm(bank[6][:, 2 * E:3 * E], ones[:, :], mask[:, 0, :], start=True, stop=False)
            mm(bank[6][:, 2 * E:3 * E], ones[:, :], mask[:, 1, :], start=False, stop=True).then_inc(rank_done, 1)
            def gather(b):
                pe.wait_ge(pick_ready, b + 1)
                for t in range(2):
                    for n in range(2):
                        last = mm(bank[3][64 * n:64 * n + 64, :], pick[:, t, :], h2[:, t, HALF * n:HALF * n + HALF],
                                  start=t == 0, stop=t == 1)
                last.then_inc(gather_done, 1)

            def transpose_xe(b):
                pe.wait_ge(xe_ready, b + 1)
                for j in range(4):
                    last = tr(bank[3][:, P * j:P * j + P], xe[:, P * j:P * j + P], ident[:, :])
                last.then_inc(xeT_done, 1)

            gather(0)
            for t in range(2):
                last = mm(bank[6][0:E, 0:1], mask[:, t, :], ones[:, 0:1], start=t == 0, stop=t == 1)
            last.then_inc(counts_done, 1)
            pe.wait_ge(gates_ready, 2)
            for t in range(2):
                last = tr(bank[7][0:E, P * t:P * t + P], gate_e2[:, t, :], ident[:, :])
            last.then_inc(gT_done, 1)
            transpose_xe(0)
            pe.wait_ge(rank_ready, 2)
            pe.wait_ge(gT_ready, 1)
            for t in range(2):
                last = tr(bank[7][0:E, P * t:P * t + P], rank_e[:, t, :], ident[:, :])
            last.then_inc(rT_done, 1)
            pe.wait_ge(blocks_ready, 1)
            mm(bank[6][0:E, 0:1], before[0:E, 0:E], blocks[:, 2:3], start=True, stop=True).then_inc(first_done, 1)

            def make_tables():
                pe.wait_ge(owner_ready, 1)
                pe.wait_ge(rT_ready, 1)
                mm(bank[6][0:1, 64:64 + NCOL], pmod[0:E, 0:1], owner, start=True, stop=True)
                mm(bank[6][0:1, 128:128 + E], blocks[:, 2:3], before[0:E, 0:E], start=True, stop=False)
                mm(bank[6][0:1, 128:128 + E], blocks[:, 2:3], ident[0:E, 0:E], start=False, stop=True)
                for t in range(2):
                    mm(bank[5][:, NCOL * t:NCOL * t + NCOL], rT[:, P * t:P * t + P], owner, start=True, stop=False)
                    mm(bank[5][:, NCOL * t:NCOL * t + NCOL], ones[0:E, :], base, start=False, stop=True)
                for t in range(2):
                    last = mm(bank[5][:, NCOL * (2 + t):NCOL * (3 + t)], gT[:, P * t:P * t + P], owner, start=True, stop=True)
                last.then_inc(tables_done, 1)

            def start_sums(t):
                pe.wait_ge(in_bdown, 16)
                if t == 0:
                    pe.wait_ge(tables_ready, 1)
                else:
                    pe.wait_ge(acc_done, 2)
                for n in range(2):
                    mm(bank[6 + n][:, :], gT[:, P * t:P * t + P], bdown[:, HALF * n:HALF * n + HALF],
                       start=True, stop=True).then_inc(part_done, 1)

            def combine(t, b, banks=(6, 7)):
                if banks == (6, 7):
                    pe.wait_ge(acc_done, b * 4 + 2 * t)
                for n in range(2):
                    mm(bank[banks[n]][:, :], combT[64 * n:64 * n + 64, t, :], y[64 * n:64 * n + 64, :],
                       start=True, stop=True).then_inc(part_done, 1)

            def block_step(b, e, is_first=False):
                pe.wait_ge(xT_ready, b + 1)
                for k in range(KC):
                    expert_chunk_here(pe, e, k)
                    w = ring[:, (EXP + k) % RING, :]
                    for half in range(2):
                        for n in range(2):
                            c0 = D * half + HALF * n
                            last = mm(bank[half][64 * n:64 * n + 64, :], xT[:, k % 4, 64 * (k // 4):64 * (k // 4) + 64],
                                      w[:, c0:c0 + HALF], start=k == 0, stop=False)
                    last.then_inc(ring_free, 1)
                    if is_first and k == 3:
                        make_tables()
                pe.wait_ge(bsel_ready, b + 1)
                for half in range(2):
                    for n in range(2):
                        c0 = D * half + HALF * n
                        last = mm(bank[half][64 * n:64 * n + 64, :], bsel, bup_parts[:, c0:c0 + HALF],
                                  start=False, stop=True)
                last.then_inc(up_done, 1)
                if is_first:
                    start_sums(0)
                else:
                    pe.wait_ge(y_ready, b)
                    pe.wait_ge(combT_ready, b)
                    combine(0, b)
                pe.wait_ge(comb_ready, b + 1)
                for t in range(2):
                    last = tr(bank[4][:, P * t:P * t + P], comb[:, t, :, :].rearrange("p a s -> p (a s)"), ident[:, :])
                last.then_inc(combT_done, 1)
                gather(b + 1)
                if is_first:
                    start_sums(1)
                else:
                    combine(1, b)
                pe.wait_ge(act_ready, b + 1)
                for j in range(2):
                    last = tr(bank[5][:, P * j:P * j + P], act[:, P * j:P * j + P], ident[:, :])
                last.then_inc(aT_low, 1)
                pe.wait_ge(combT_ready, b + 1)
                for j in range(2):
                    last = tr(bank[4][:, P * j:P * j + P], act[:, P * (2 + j):P * (2 + j) + P], ident[:, :])
                last.then_inc(aT_high, 1)
                transpose_xe(b + 1)
                pe.wait_ge(aT_dve, b + 1)
                pe.wait_ge(aT_act, b + 1)
                for k in range(KC):
                    if k % 2 == 0:
                        expert_chunk_here(pe, e, KC + k // 2)
                    w = ring[:, (EXP + KC + k // 2) % RING, D * (k % 2):D * (k % 2) + D]
                    half, j = k // 4, k % 4
                    for n in range(2):
                        last = mm(bank[2][64 * n:64 * n + 64, :], aT[:, j, 64 * half:64 * half + 64],
                                  w[:, HALF * n:HALF * n + HALF], start=k == 0, stop=k == KC - 1)
                    if k % 2 == 1:
                        last.then_inc(ring_free, 1)

            pe.wait_ge(bup_split, 1)
            block_step(0, 0, is_first=True)
            last_block = number_of_blocks(pe)
            with pe.Fori(1, last_block) as b:
                e = pe.value_load(whose_i[0:1, bass.ds(b, 1)], min_val=0, max_val=E - 1)
                block_step(b, e)
            pe.wait_ge(y_ready, last_block)
            pe.wait_ge(combT_ready, last_block)
            combine(0, last_block, LAST_BANKS[0])
            combine(1, last_block, LAST_BANKS[1])


_INS = ["x", "c", "ctx", "c_ctx", "ada_w", "ada_b", "norm_g", "na_w_qkv", "na_w_o", "na_rpb", "moe_w_router",
        "moe_b_router", "moe_w_up", "moe_b_up", "moe_w_down", "moe_b_down"]


def kernel(**inputs):
    import concourse.bacc as bacc
    from concourse.bass_utils import run_bass_kernel_spmd

    nc = bacc.Bacc("TRN2", target_bir_lowering=False, num_devices=1)
    arrays, args = {}, []
    for name in _INS:
        a = np.ascontiguousarray(inputs[name])
        arrays[f"in_{name}"] = a
        args.append(nc.dram_tensor(f"in_{name}", a.shape, mybir.dt.from_np(a.dtype), kind="ExternalInput").ap())
    args.append(nc.dram_tensor("out_x", (1, TOK, D), F32, kind="ExternalOutput").ap())
    build(nc, *args)
    r = run_bass_kernel_spmd(nc, [arrays], core_ids=[0])
    return r.results[0]["out_x"]
```
